# Optimizing a Trainium2 kernel written in Bass

```python
import math
import jax, jax.numpy as jnp
from jax import lax
import numpy as np

D_MODEL = 1024
BATCH = 1
SEQ = 256
DEPTH = 1

D_PLE = 256
D_ATTN = D_MODEL // 2
HEAD_DIM = 64
N_ATTN_HEADS = D_ATTN // HEAD_DIM
D_POOL = D_MODEL - D_ATTN
POOL_WINDOWS = (2, 4, 8, 16)
N_POOL_GROUPS = len(POOL_WINDOWS)
POOL_GROUP_DIM = D_POOL // N_POOL_GROUPS
D_MIX = D_ATTN + D_POOL
D_IN_PROJ = 3 * D_ATTN + D_POOL
MOBA_BLOCK = 256
MOBA_TOPK = 3
Q_CHUNK = 64
REL_BUCKETS = 32
REL_MAX_DIST = 128
N_EXPERT_GROUPS = 4
EXPERTS_PER_GROUP = 8
D_EXPERT = 512
TOP_K_INNER = 2
RMS_EPS = 1e-6

kernel_name = "hymba_moba_pool_hiermoe_block"

def rms_norm(x, g):
    xf = x.astype(jnp.float32)
    y = xf * lax.rsqrt(jnp.mean(xf * xf, axis=-1, keepdims=True) + RMS_EPS)
    return (y * g.astype(jnp.float32)).astype(x.dtype)

def rel_bucket(n):
    n = jnp.maximum(n, 0)
    max_exact = REL_BUCKETS // 2
    nf = jnp.maximum(n, 1).astype(jnp.float32)
    large = max_exact + (jnp.log(nf / max_exact) / math.log(REL_MAX_DIST / max_exact)
                         * (REL_BUCKETS - max_exact)).astype(jnp.int32)
    large = jnp.minimum(large, REL_BUCKETS - 1)
    return jnp.where(n < max_exact, n, large)

def moba_attention(q, k, v, rel_bias):
    B, S, H, hd = q.shape
    nb = -(-S // MOBA_BLOCK)
    s_pad = nb * MOBA_BLOCK
    pad = ((0, 0), (0, s_pad - S), (0, 0), (0, 0))
    q, k, v = (jnp.pad(t, pad).transpose(0, 2, 1, 3) for t in (q, k, v))
    kb = k.reshape(B, H, nb, MOBA_BLOCK, hd)
    vb = v.reshape(B, H, nb, MOBA_BLOCK, hd)
    kmean = jnp.mean(kb.astype(jnp.float32), axis=3)
    k_sel = min(MOBA_TOPK, max(nb - 1, 1))
    scale = HEAD_DIM ** -0.5
    bias_ht = rel_bias.T.astype(jnp.float32)
    n_chunks = s_pad // Q_CHUNK
    qc = jnp.moveaxis(q.reshape(B, H, n_chunks, Q_CHUNK, hd), 2, 0)
    b_ix = jnp.arange(B)[:, None, None, None]
    h_ix = jnp.arange(H)[None, :, None, None]
    h_ix5 = h_ix[..., None]
    blk_ar = jnp.arange(MOBA_BLOCK)

    def chunk_fn(args):
        ci, q_c = args
        q0 = ci * Q_CHUNK
        ob = q0 // MOBA_BLOCK
        q_pos = q0 + jnp.arange(Q_CHUNK)
        qf = q_c.astype(jnp.float32)
        gate = jnp.einsum('bhqd,bhnd->bhqn', qf, kmean)
        gate = jnp.where(jnp.arange(nb) < ob, gate, -jnp.inf)
        _, idx = lax.top_k(gate, k_sel)
        valid = idx < ob
        k_g = kb[b_ix, h_ix, idx].astype(jnp.float32)
        v_g = vb[b_ix, h_ix, idx].astype(jnp.float32)
        s_sel = jnp.einsum('bhqd,bhqknd->bhqkn', qf, k_g) * scale
        key_pos_sel = idx[..., None] * MOBA_BLOCK + blk_ar
        bucket_sel = rel_bucket(q_pos[None, None, :, None, None] - key_pos_sel)
        s_sel = s_sel + bias_ht[h_ix5, bucket_sel]
        s_sel = jnp.where(valid[..., None], s_sel, -jnp.inf)
        k_own = lax.dynamic_index_in_dim(kb, ob, axis=2, keepdims=False).astype(jnp.float32)
        v_own = lax.dynamic_index_in_dim(vb, ob, axis=2, keepdims=False).astype(jnp.float32)
        dist_own = q_pos[:, None] - (ob * MOBA_BLOCK + blk_ar)[None, :]
        s_own = (jnp.einsum('bhqd,bhnd->bhqn', qf, k_own) * scale
                 + bias_ht[:, rel_bucket(dist_own)])
        s_own = jnp.where(dist_own >= 0, s_own, -jnp.inf)
        logits = jnp.concatenate(
            [s_sel.reshape(B, H, Q_CHUNK, k_sel * MOBA_BLOCK), s_own], axis=-1)
        probs = jax.nn.softmax(logits, axis=-1)
        p_sel = probs[..., :k_sel * MOBA_BLOCK].reshape(B, H, Q_CHUNK, k_sel, MOBA_BLOCK)
        p_own = probs[..., k_sel * MOBA_BLOCK:]
        out = (jnp.einsum('bhqkn,bhqknd->bhqd', p_sel, v_g)
               + jnp.einsum('bhqn,bhnd->bhqd', p_own, v_own))
        return out.astype(q_c.dtype)

    out = lax.map(chunk_fn, (jnp.arange(n_chunks, dtype=jnp.int32), qc))
    out = out.transpose(1, 0, 3, 2, 4).reshape(B, s_pad, H * hd)
    return out[:, :S]

def causal_pool_mixer(u, w_pool, pool_scale):
    B, S, _ = u.shape
    uf = u.astype(jnp.float32)
    cs = jnp.concatenate([jnp.zeros((B, 1, D_POOL), jnp.float32), jnp.cumsum(uf, axis=1)], axis=1)
    t = jnp.arange(S)
    means = []
    for gi, w in enumerate(POOL_WINDOWS):
        c = cs[..., gi * POOL_GROUP_DIM:(gi + 1) * POOL_GROUP_DIM]
        start = jnp.maximum(t + 1 - w, 0)
        cnt = (t + 1 - start).astype(jnp.float32)[None, :, None]
        means.append((c[:, 1:] - c[:, start]) / cnt)
    pooled = (jnp.concatenate(means, axis=-1) - uf).reshape(B, S, N_POOL_GROUPS, POOL_GROUP_DIM)
    y = jnp.einsum('bsgc,gcd->bsgd', pooled, w_pool.astype(jnp.float32)).reshape(B, S, D_POOL)
    return (y * pool_scale.astype(jnp.float32)).astype(u.dtype)

def hier_moe(h, w_r1, b_r1, w_r2, b_r2, w_gate, w_up, w_down):
    B, S, D = h.shape
    hf = h.reshape(-1, D)
    logits1 = jnp.dot(hf, w_r1).astype(jnp.float32) + b_r1.astype(jnp.float32)
    p1 = jax.nn.softmax(logits1, axis=-1)
    g_sel = jnp.argmax(logits1, axis=-1)
    p_g = jnp.take_along_axis(p1, g_sel[:, None], axis=-1)[:, 0]
    logits2 = (jnp.einsum('td,gde->tge', hf, w_r2).astype(jnp.float32)
               + b_r2.astype(jnp.float32))
    l2 = jnp.take_along_axis(logits2, g_sel[:, None, None], axis=1)[:, 0]
    top_v, top_i = lax.top_k(l2, TOP_K_INNER)
    w2 = jax.nn.softmax(top_v, axis=-1)
    inner = jnp.sum(jax.nn.one_hot(top_i, EXPERTS_PER_GROUP, dtype=jnp.float32) * w2[..., None], axis=1)
    gates = (jax.nn.one_hot(g_sel, N_EXPERT_GROUPS, dtype=jnp.float32)[:, :, None]
             * (p_g[:, None] * inner)[:, None, :])
    y = jnp.zeros(hf.shape, jnp.float32)
    for g in range(N_EXPERT_GROUPS):
        a = jnp.einsum('td,edf->tef', hf, w_gate[g])
        u = jnp.einsum('td,edf->tef', hf, w_up[g])
        hid = (jax.nn.silu(a.astype(jnp.float32)) * u.astype(jnp.float32)
               * gates[:, g, :, None])
        y = y + jnp.einsum('tef,efd->td', hid.astype(h.dtype), w_down[g]).astype(jnp.float32)
    return y.astype(h.dtype).reshape(B, S, D)

def setup_inputs(seed: int = 0) -> dict:
    key = jax.random.key(seed)
    ks = jax.random.split(key, 24)
    f32 = jnp.float32
    nrm = lambda k, shape, s: jax.random.normal(k, shape, f32) * s
    L, G, E = DEPTH, N_EXPERT_GROUPS, EXPERTS_PER_GROUP
    return {
        "x": nrm(ks[0], (BATCH, SEQ, D_MODEL), 1.0),
        "p": nrm(ks[1], (DEPTH, BATCH, SEQ, D_PLE), 1.0),
        "g_mix": 1.0 + nrm(ks[2], (L, D_MODEL), 0.05),
        "w_in": nrm(ks[3], (L, D_MODEL, D_IN_PROJ), D_MODEL ** -0.5),
        "w_pool": nrm(ks[4], (L, N_POOL_GROUPS, POOL_GROUP_DIM, POOL_GROUP_DIM), POOL_GROUP_DIM ** -0.5),
        "pool_scale": 1.0 + nrm(ks[5], (L, D_POOL), 0.1),
        "w_out": nrm(ks[6], (L, D_MIX, D_MODEL), D_MIX ** -0.5),
        "rel_bias": nrm(ks[7], (REL_BUCKETS, N_ATTN_HEADS), 0.5),
        "g_ffn": 1.0 + nrm(ks[8], (L, D_MODEL), 0.05),
        "w_r1": nrm(ks[9], (L, D_MODEL, G), D_MODEL ** -0.5),
        "b_r1": nrm(ks[10], (L, G), 0.01),
        "w_r2": nrm(ks[11], (L, G, D_MODEL, E), D_MODEL ** -0.5),
        "b_r2": nrm(ks[12], (L, G, E), 0.01),
        "w_gate": nrm(ks[13], (L, G, E, D_MODEL, D_EXPERT), D_MODEL ** -0.5),
        "w_up": nrm(ks[14], (L, G, E, D_MODEL, D_EXPERT), D_MODEL ** -0.5),
        "w_down": nrm(ks[15], (L, G, E, D_EXPERT, D_MODEL), D_EXPERT ** -0.5),
        "g_ple": 1.0 + nrm(ks[16], (L, D_MODEL), 0.05),
        "w_ple_proj": nrm(ks[17], (L, D_PLE, D_MODEL), D_PLE ** -0.5),
        "w_ple_gate": nrm(ks[18], (L, D_MODEL, D_MODEL), D_MODEL ** -0.5),
        "g_final": 1.0 + nrm(ks[19], (D_MODEL,), 0.05),
    }

def reference(x, p, g_mix, w_in, w_pool, pool_scale, w_out, rel_bias, g_ffn, w_r1, b_r1,
              w_r2, b_r2, w_gate, w_up, w_down, g_ple, w_ple_proj, w_ple_gate, g_final):
    B, S, _ = x.shape
    for i in range(DEPTH):
        h = rms_norm(x, g_mix[i])
        z = jnp.dot(h, w_in[i])
        q = z[..., :D_ATTN].reshape(B, S, N_ATTN_HEADS, HEAD_DIM)
        k = z[..., D_ATTN:2 * D_ATTN].reshape(B, S, N_ATTN_HEADS, HEAD_DIM)
        v = z[..., 2 * D_ATTN:3 * D_ATTN].reshape(B, S, N_ATTN_HEADS, HEAD_DIM)
        u = z[..., 3 * D_ATTN:]
        a = moba_attention(q, k, v, rel_bias)
        b = causal_pool_mixer(u, w_pool[i], pool_scale[i])
        x = x + jnp.dot(jnp.concatenate([a, b], axis=-1), w_out[i])
        x = x + hier_moe(rms_norm(x, g_ffn[i]), w_r1[i], b_r1[i], w_r2[i], b_r2[i],
                         w_gate[i], w_up[i], w_down[i])
        gate = jax.nn.sigmoid(jnp.dot(rms_norm(x, g_ple[i]), w_ple_gate[i]).astype(jnp.float32))
        x = x + (jnp.dot(p[i], w_ple_proj[i]).astype(jnp.float32) * gate).astype(x.dtype)
    return rms_norm(x, g_final)


_drawn_inputs = setup_inputs


def setup_inputs(seed=0):
    import zlib

    import numpy as np

    out = dict(_drawn_inputs(seed))
    spreads = {}
    factors = {'b_r1': 8.0, 'b_r2': 3.13, 'g_ple': 7.163}
    for name, (base, spread) in spreads.items():
        noise = np.random.default_rng([zlib.crc32(name.encode()), seed]).standard_normal(out[name].shape)
        drawn = base * np.exp(spread * noise) if base else spread * noise
        out[name] = __import__('jax').numpy.asarray(drawn.astype(out[name].dtype))
    for name, factor in factors.items():
        out[name] = (out[name] * factor).astype(out[name].dtype)
    return out
```

```python
from contextlib import ExitStack

import numpy as np

import concourse.bass as bass
from concourse import mybir

F32 = mybir.dt.float32
I32 = mybir.dt.int32
ALU = mybir.AluOpType
ACT = mybir.ActivationFunctionType
AX = mybir.AxisListType.X

P = 128
SEQ = 256
TILES = SEQ // P
D = 1024
HEADS, HEAD_DIM = 8, 64
D_ATTN = HEADS * HEAD_DIM
GROUPS, GROUP_EXPERTS, D_EXPERT = 4, 8, 512
EXPERTS = GROUPS * GROUP_EXPERTS
QUAD = 4
SLOTS = 32
QUADS_PER_STEP = 2
STEPS = EXPERTS // QUAD // QUADS_PER_STEP
PASSES = SEQ // SLOTS
D_PLE = 256
POOL_WINDOWS = (2, 4, 8, 16)
POOL_GROUPS = len(POOL_WINDOWS)
PAD = 16
BUCKETS, MAX_DIST = 32, 128
EPS = 1e-6
MASKED = -1e30
RING = 8
UNIT = 4096
W_IN_UNITS, W_OUT_UNITS, QUAD_UNITS = 4, 2, 12
FIRST_EXPERT_UNIT = W_IN_UNITS + W_OUT_UNITS
STEP_UNITS = QUADS_PER_STEP * QUAD_UNITS
STEP_USES = STEP_UNITS // RING
EXPERT_UNITS = STEPS * STEP_UNITS
BIAS_ROW = 384
NO_SLOT = 1000.0

C_IDENT, C_EARLIER, C_ONES, C_SLOT, C_FIRST, C_EDGE = 0, 128, 256, 384, 416, 448
C_KEPT = C_EDGE + POOL_GROUPS * PAD
C_FLIP, C_BUCKET = 0, 128
C_EARLY = 384


def layer_kernel(nc, a, out):
    with ExitStack() as ctx:
        def sbuf(name, cols, dt=F32, rows=P):
            return ctx.enter_context(nc.sbuf_tensor(name, [rows, cols], dt))

        def sem(name):
            return ctx.enter_context(nc.semaphore(name))

        ring = ctx.enter_context(nc.sbuf_tensor("ring", [P, RING, UNIT], F32))
        x_sb = ctx.enter_context(nc.sbuf_tensor("x_sb", [P, TILES, D], F32))
        h_sb = ctx.enter_context(nc.sbuf_tensor("h_sb", [P, TILES, D], F32))
        hT = ctx.enter_context(nc.sbuf_tensor("hT", [P, 8, SEQ], F32))
        qk_area = sbuf("qk_area", 2048)
        v_area = sbuf("v_area", 1024)
        bias_area = sbuf("bias_area", 2048)
        pool_area = sbuf("pool_area", 3 * POOL_GROUPS * (SEQ + PAD))
        attn_area = sbuf("attn_area", 2304)
        gain = sbuf("gain", D)
        consts = sbuf("consts", C_KEPT)
        w_pool = ctx.enter_context(nc.sbuf_tensor("w_pool_sb", [P, POOL_GROUPS, P], F32))
        pool_scale = sbuf("pool_scale_sb", POOL_GROUPS)
        router = ctx.enter_context(nc.sbuf_tensor("router", [P, 8, GROUPS + EXPERTS], F32))
        router_bias = sbuf("router_bias", GROUPS + EXPERTS)
        rel_bias = sbuf("rel_bias_sb", HEADS, rows=BUCKETS)
        eps = sbuf("eps", 1)
        sum_sq = sbuf("sum_sq", 8)
        root = sbuf("root", 8)
        rstd = sbuf("rstd", 8)
        row_max = ctx.enter_context(nc.sbuf_tensor("row_max", [P, HEADS, TILES], F32))
        neg_max = ctx.enter_context(nc.sbuf_tensor("neg_max", [P, HEADS, TILES], F32))
        row_sum = ctx.enter_context(nc.sbuf_tensor("row_sum", [P, TILES, HEADS], F32))
        row_inv = ctx.enter_context(nc.sbuf_tensor("row_inv", [P, TILES, HEADS], F32))
        routing = sbuf("routing", 12 * TILES * EXPERTS)
        tiny = ctx.enter_context(nc.sbuf_tensor("tiny", [P, 16, TILES], F32))
        ranks = ctx.enter_context(nc.sbuf_tensor("ranks", [P, TILES, EXPERTS], F32))
        most = sbuf("most", 1)
        most_int = sbuf("most_int", 1, I32)

        ident = consts[:, C_IDENT:C_IDENT + P]
        earlier = consts[:, C_EARLIER:C_EARLIER + P]
        ones = consts[:, C_ONES:C_ONES + P]
        slot_no = consts[:, C_SLOT:C_SLOT + SLOTS]
        first = consts[:, C_FIRST:C_FIRST + EXPERTS]
        edge = consts[:, C_EDGE:C_KEPT].rearrange("p (g t) -> p g t", g=POOL_GROUPS)

        small = routing[:, :].rearrange("p (i t e) -> p i t e", i=12, t=TILES)
        r1_sb = routing[:, 0:32].rearrange("p (i c g) -> p i c g", i=4, c=2)
        r2_sb = routing[:, 32:288].rearrange("p (g i c) -> p g i c", g=GROUPS, i=4)

        qT = qk_area[:, 0:1024].rearrange("p (c t) -> p c t", c=4)
        kT = qk_area[:, 1024:2048].rearrange("p (c t) -> p c t", c=4)
        ple = qk_area[:, :].rearrange("p (t n) -> p t n", t=TILES)
        flip = v_area[:, C_FLIP:C_FLIP + P]
        bucket_of = v_area[0:BUCKETS, C_BUCKET:C_BUCKET + SEQ]
        bias_row = v_area[0:HEADS, C_EARLY:C_EARLY + BIAS_ROW]
        v_sb = v_area[:, :].rearrange("p (t n) -> p t n", t=TILES)
        down_sb = v_area[:, :]
        bias_of = bias_area[:, :].rearrange("p (h k) -> p h k", h=HEADS)
        xT = bias_area[:, 0:1024].rearrange("p (c s) -> p c s", c=8)
        hidden = bias_area[:, 1024:1536]
        hiddenT = bias_area[:, 1536:2048].rearrange("p (c s) -> p c s", c=4)
        width = POOL_GROUPS * (SEQ + PAD)
        u_pad, sum_a, sum_b = (pool_area[:, i * width:(i + 1) * width].rearrange("p (g t) -> p g t", g=POOL_GROUPS)
                               for i in range(3))
        select = pool_area[:, 0:256].rearrange("p (t e s) -> p t e s", t=TILES, e=QUAD)
        weighted = pool_area[:, 256:512].rearrange("p (t e s) -> p t e s", t=TILES, e=QUAD)
        scatterT = pool_area[:, 512:768]
        g_ple = pool_area[:, 768:1792]
        g_final = pool_area[:, 1792:2816]
        flipped = attn_area[:, 0:2048].rearrange("p (h k) -> p h k", h=HEADS)
        scores = [attn_area[:, 384 * i:384 * i + 384] for i in range(2)]
        probs = [attn_area[:, 768 + 384 * i:768 + 384 * i + 384] for i in range(2)]
        probsT = [attn_area[:, 1536 + 384 * i:1536 + 384 * i + 384] for i in range(2)]
        silu = attn_area[:, 0:512]
        p_sb = attn_area[:, 512:1024].rearrange("p (t n) -> p t n", t=TILES)
        pT = attn_area[:, 1024:1536].rearrange("p (c t) -> p c t", c=2)
        mixT = hT

        psum = ctx.enter_context(nc.psum_tensor("psum", [P, 8, 512], F32))

        bias_dram = nc.dram_tensor("bias_by_distance", [HEADS, BIAS_ROW], F32, kind="Internal").ap()

        x_in = [sem(f"x_in{t}") for t in range(TILES)]
        consts_in, early_in, gain_in, small_in, route_in = map(
            sem, ("consts_in", "early_in", "gain_in", "small_in", "route_in"))
        bias_out, bias_in, tail_in, p_in, out_done = map(sem, ("bias_out", "bias_in", "tail_in", "p_in", "out_done"))
        slot_in = [sem(f"slot_in{s}") for s in range(RING)]
        more_in = [sem(f"more_in{s}") for s in range(RING)]
        ring_free, more_free = sem("ring_free"), sem("more_free")
        vec = sem("vector_step")
        squared, rooted, normed, turned_ps, turned_act, turned_vec = map(
            sem, ("squared", "rooted", "normed", "turned_ps", "turned_act", "turned_vec"))
        summed = sem("summed")
        bias_ps, bias_sb_ok, flipped_ps, bias_ready = map(sem, ("bias_ps", "bias_row_ready", "flipped_ps", "bias_ready"))
        z_ps, z_act, z_vec = map(sem, ("z_ps", "z_act", "z_vec"))
        pooled, pool_step, pool_ps, pool_done, padded = map(
            sem, ("pooled", "pool_step", "pool_ps", "pool_done", "padded"))
        router_ready = sem("router_ready")
        scores_ps, scored, exped, probs_ps, probs_sb = map(
            sem, ("scores_ps", "scored", "exped", "probs_ps", "probs_sb"))
        attn_ps, attn_sb, attnT_ps, attnT_sb, mix_ps = map(
            sem, ("attn_ps", "attn_sb", "attnT_ps", "attnT_sb", "mix_ps"))
        logits_ps, exp_in, exp_out, chosen, rank_ps, routed = map(
            sem, ("logits_ps", "exp_in", "exp_out", "chosen", "rank_ps", "routed"))
        pT_ps, pT_sb, ple_ps, ple_sb = map(sem, ("pT_ps", "pT_sb", "ple_ps", "ple_sb"))
        open_ps, opened, final_x, final_out, added = map(
            sem, ("gate_logits_ps", "gate_opened", "final_x", "final_out", "added"))

        names = ("sel_ready", "gath_ps", "xT_act", "xT_vec", "scat_ps", "scat_sb", "gate_ps", "silu_ready", "up_ps",
                 "hid_ready", "hidT_ps", "hidT_sb", "down_ps", "down_act", "down_vec", "sel_step")
        main_s = {n: sem("m_" + n) for n in names}
        more_s = {n: sem("o_" + n) for n in names}
        next_ranks = sem("next_ranks")

        w_in = a["w_in"][0].rearrange("(i p c) n -> i p (c n)", i=W_IN_UNITS, c=2)
        w_out = a["w_out"][0].rearrange("(i c p) n -> i p c n", i=W_OUT_UNITS, c=4)
        w_ple_gate = a["w_ple_gate"][0].rearrange("(i c p) n -> i p c n", i=2, c=4)
        w_ple = a["w_ple_proj"][0].rearrange("(c p) n -> p c n", p=P)
        w_gate, w_up = (a[n][0].rearrange("g (q e) (i p c) f -> (g q) i p e (c f)", e=QUAD, p=P, c=2)
                        for n in ("w_gate", "w_up"))
        w_down = a["w_down"][0].rearrange("g (q e) (i p) n -> (g q) i p e n", e=QUAD, p=P)
        x_dram = a["x"][0].rearrange("(t p) n -> t p n", p=P)
        out_dram = out[0].rearrange("(t p) n -> t p n", p=P)
        p_dram = a["p"][0, 0].rearrange("(t p) n -> p t n", p=P)

        def broadcast(row):
            return row.rearrange("(o n) -> o n", o=1).broadcast_to([P, row.shape[0]])

        def unit(slot):
            return ring[:, slot, :]

        def expert_unit(slot):
            return unit(slot).rearrange("p (e n) -> p e n", e=QUAD)

        def norm_cols(which, t):
            return 2 * which + t

        block = ctx.enter_context(nc.Block())

        @block.sync
        def _(sp):
            for t in range(TILES):
                sp.dma_start(x_sb[:, t, :], x_dram[t]).then_inc(x_in[t], 16)
            sp.sem_inc(ring_free, RING)
            for i in range(W_IN_UNITS):
                sp.dma_start(unit(i), w_in[i]).then_inc(slot_in[i], 16)
            for i in range(W_OUT_UNITS):
                s = W_IN_UNITS + i
                sp.dma_start(unit(s).rearrange("p (c n) -> p c n", c=4), w_out[i]).then_inc(slot_in[s], 16)

            def load_step(step, quad0, arrived, free, already):
                for u in range(STEP_UNITS):
                    q, i = divmod(u, QUAD_UNITS)
                    kind, part = divmod(i, 4)
                    w = (w_gate, w_up, w_down)[kind]
                    slot = (FIRST_EXPERT_UNIT + u) % RING
                    sp.wait_ge(free, step * STEP_UNITS + already + u + 1)
                    sp.dma_start(expert_unit(slot), w[bass.ds(quad0 + q, 1), part][0]).then_inc(arrived[slot], 16)

            with sp.Fori(0, STEPS) as step:
                load_step(step, step * QUADS_PER_STEP, slot_in, ring_free, FIRST_EXPERT_UNIT)

            sp.wait_ge(routed, 1)
            with sp.If(sp.value_load(most_int[0:1, 0:1], min_val=0, max_val=SEQ) > SLOTS):
                sp.wait_ge(ring_free, RING + FIRST_EXPERT_UNIT + EXPERT_UNITS)
                sp.sem_inc(more_free, RING)
                with sp.Fori(0, PASSES - 1) as again:
                    with sp.Fori(0, STEPS) as step:
                        load_step(again * STEPS + step, step * QUADS_PER_STEP, more_in, more_free, 0)
                sp.wait_ge(more_free, RING + (PASSES - 1) * EXPERT_UNITS)
            for i in range(3):
                n = FIRST_EXPERT_UNIT + EXPERT_UNITS + i
                sp.wait_ge(ring_free, n + 1)
                if i < 2:
                    sp.dma_start(unit(n % RING).rearrange("p (c n) -> p c n", c=4),
                                 w_ple_gate[i]).then_inc(slot_in[n % RING], 16)
                else:
                    sp.dma_start(unit(n % RING)[:, 0:2048].rearrange("p (c n) -> p c n", c=2),
                                 w_ple).then_inc(slot_in[n % RING], 16)
            for t in range(TILES):
                sp.wait_ge(final_out, t + 1)
                sp.dma_start(out_dram[t], h_sb[:, t, :]).then_inc(out_done, 16)
            sp.wait_ge(out_done, 16 * TILES)

        @block.scalar
        def _(act):
            act.dma_start(consts[:, :], a["consts"][:, 0:C_KEPT]).then_inc(consts_in, 16)
            act.dma_start(gain[:, :], broadcast(a["g_mix"][0])).then_inc(gain_in, 16)
            act.dma_start(v_area[:, 0:C_EARLY], a["consts"][:, C_KEPT:C_KEPT + C_EARLY]).then_inc(early_in, 16)
            act.dma_start(rel_bias[:, :], a["rel_bias"]).then_inc(early_in, 16)

            def root_mean_square(which, t, source, scratch, ready, at):
                act.wait_ge(ready, at)
                act.activation(scratch, source, ACT.Square, accum_out=sum_sq[:, norm_cols(which, t):][:, 0:1]
                               ).then_inc(squared, 1)
                act.wait_ge(squared, norm_cols(which, t) + 1)
                if which == 0 and t == 0:
                    act.wait_ge(vec, 1)
                c = norm_cols(which, t)
                act.activation(root[:, c:c + 1], sum_sq[:, c:c + 1], ACT.Sqrt, scale=1.0 / D,
                               bias=eps[:, 0:1]).then_inc(rooted, 1)

            for t in range(TILES):
                root_mean_square(0, t, x_sb[:, t, :], h_sb[:, t, :], x_in[t], 16)

            act.dma_start(w_pool[:, :, :], a["w_pool"][0].rearrange("g c d -> c g d")).then_inc(small_in, 16)
            with nc.allow_non_contiguous_dma(reason="512 single values"):
                act.dma_start(pool_scale[:, :], a["pool_scale"][0].rearrange("(g d) -> d g", d=P)).then_inc(small_in, 16)
                act.dma_start(r1_sb[:, :, :, :], a["w_r1"][0].rearrange("(i p c) g -> p i c g", i=4, c=2)
                              ).then_inc(route_in, 16)
                for g in range(GROUPS):
                    act.dma_start(r2_sb[:, g, :, :], a["w_r2"][0, g].rearrange("(i p c) e -> p i (c e)", i=4, c=2)
                                  ).then_inc(route_in, 16)
            act.dma_start(router_bias[:, 0:GROUPS], broadcast(a["b_r1"][0])).then_inc(route_in, 16)
            act.dma_start(router_bias[:, GROUPS:], broadcast(a["b_r2"][0].rearrange("g e -> (g e)"))
                          ).then_inc(route_in, 16)
            act.wait_ge(bias_sb_ok, 2)
            act.dma_start(bias_dram[:, :], bias_row).then_inc(bias_out, 16)
            act.wait_ge(bias_out, 16)
            skewed = bass.AP(tensor=bias_dram.tensor, offset=0, ap=[[1, P], [BIAS_ROW, HEADS], [1, SEQ]])
            act.dma_start(flipped, skewed).then_inc(bias_in, 16)
            act.wait_ge(normed, 2)
            act.dma_start(gain[:, :], broadcast(a["g_ffn"][0])).then_inc(gain_in, 16)

            def turned_out(which, t, half, bank, dest):
                act.wait_ge(turned_ps, 4 * which + 2 * t + half + 1)
                act.copy(dest[:, 4 * half:4 * half + 4, t * P:(t + 1) * P],
                         psum[:, bank, :].rearrange("p (c s) -> p c s", c=4)).then_inc(turned_act, 1)

            for t in range(TILES):
                turned_out(0, t, 0, 2 * t, hT)

            for b in range(2):
                act.wait_ge(z_ps, b + 1)
                act.copy(u_pad[:, 2 * b:2 * b + 2, PAD:], psum[:, 4 + b, :].rearrange("p (c t) -> p c t", c=2)
                         ).then_inc(z_act, 1)
            for b in range(2):
                act.wait_ge(z_ps, 2 * b + 4)
                act.copy(kT[:, 2 * b:2 * b + 2, :], psum[:, 2 + b, :].rearrange("p (c t) -> p c t", c=2)
                         ).then_inc(z_act, 1)
            act.wait_ge(z_ps, 8)
            act.copy(v_sb[:, 1, :], psum[:, 7, :]).then_inc(z_act, 1)

            for h in range(HEADS):
                act.wait_ge(scored, h + 1)
                if h >= 2:
                    act.wait_ge(probs_ps, h - 1)
                for t in range(TILES):
                    lo, hi = (0, 128) if t == 0 else (128, 384)
                    act.activation(probs[h % 2][:, lo:hi], scores[h % 2][:, lo:hi], ACT.Exp,
                                   bias=neg_max[:, h, t:t + 1], accum_out=row_sum[:, t, h:h + 1]).then_inc(exped, 1)
                if h >= 2:
                    act.wait_ge(attn_ps, h - 1)
                act.wait_ge(probs_ps, h + 1)
                act.copy(probsT[h % 2], psum[:, 6, 0:384]).then_inc(probs_sb, 1)
                if h % 4 == 3:
                    act.wait_ge(attnT_ps, h // 4 + 1)
                    act.copy(mixT[:, 2 * (h // 4):2 * (h // 4) + 2, :],
                             psum[:, 6, :].rearrange("p (c t) -> p c t", c=2)).then_inc(attnT_sb, 1)
            for t in range(TILES):
                root_mean_square(1, t, h_sb[:, t, :], v_area[:, 0:1024], summed, t + 1)
            act.wait_ge(mix_ps, 2)
            act.dma_start(g_ple, broadcast(a["g_ple"][0])).then_inc(tail_in, 16)
            act.dma_start(g_final, broadcast(a["g_final"])).then_inc(tail_in, 16)
            act.dma_start(p_sb, p_dram).then_inc(p_in, 16)
            for t in range(TILES):
                turned_out(1, t, 0, 4 + 2 * t, hT)
            for n in range(2):
                act.wait_ge(exp_in, n + 1)
                if n == 0:
                    shifted = small[:, 1, :, 0:GROUPS]
                    act.activation(small[:, 2, :, 0:GROUPS], shifted, ACT.Exp).then_inc(exp_out, 1)
                else:
                    act.activation(tiny[:, 6, :], tiny[:, 5, :], ACT.Exp).then_inc(exp_out, 1)

            def moe_step(step, s):
                for q in range(QUADS_PER_STEP):
                    n = step * QUADS_PER_STEP + q
                    act.wait_ge(s["gath_ps"], n * 2 + 1)
                    act.copy(xT[:, 0:4, :], psum[:, 6, :].rearrange("p (c s) -> p c s", c=4)).then_inc(s["xT_act"], 1)
                    act.wait_ge(s["gate_ps"], n + 1)
                    act.activation(silu, psum[:, 4, :], ACT.Silu).then_inc(s["silu_ready"], 1)
                    act.wait_ge(s["hidT_ps"], n + 1)
                    act.copy(hiddenT[:, :, :], psum[:, 4, :].rearrange("p (c s) -> p c s", c=4)
                             ).then_inc(s["hidT_sb"], 1)
                    act.wait_ge(s["down_ps"], n + 1)
                    act.copy(down_sb[:, 0:512], psum[:, 6, :]).then_inc(s["down_act"], 1)

            with act.Fori(0, STEPS) as step:
                moe_step(step, main_s)
            act.wait_ge(routed, 1)
            with act.If(act.value_load(most_int[0:1, 0:1], min_val=0, max_val=SEQ) > SLOTS):
                with act.Fori(0, PASSES - 1) as again:
                    with act.Fori(0, STEPS) as step:
                        moe_step(again * STEPS + step, more_s)
                act.nop()
            act.wait_ge(pT_ps, 1)
            act.copy(pT[:, :, :], psum[:, 4, :].rearrange("p (c t) -> p c t", c=2)).then_inc(pT_sb, 1)
            root_mean_square(2, 0, x_sb[:, 0, :], v_area[:, 0:1024], summed, 3)
            root_mean_square(2, 1, x_sb[:, 1, :], bias_area[:, 0:1024], summed, 4)
            for b in range(2):
                act.wait_ge(ple_ps, b + 1)
                act.copy(ple[:, b, :].rearrange("p (b n) -> p b n", b=2), psum[:, 4 + 2 * b:6 + 2 * b, :]
                         ).then_inc(ple_sb, 1)
            for t in range(TILES):
                turned_out(2, t, 0, 2 * t, hT)
            for t in range(TILES):
                act.wait_ge(open_ps, t + 1)
                act.activation(h_sb[:, t, :].rearrange("p (b n) -> p b n", b=2), psum[:, 4 + 2 * t:6 + 2 * t, :],
                               ACT.Sigmoid).then_inc(opened, 1)
            for t in range(TILES):
                root_mean_square(3, t, x_sb[:, t, :], (v_area, bias_area)[t][:, 0:1024], final_x, t + 1)

        @block.gpsimd
        def _(pool):
            pool.memset(pool_area[:, :].rearrange("p (g t) -> p g t", g=3 * POOL_GROUPS)[:, :, 0:PAD], 0.0
                        ).then_inc(padded, 1)
            pool.wait_ge(route_in, 16 * (3 + GROUPS))
            pool.tensor_copy(router[:, :, 0:GROUPS], r1_sb[:, :, :, :].rearrange("p i c g -> p (i c) g")
                             ).then_inc(router_ready, 1)
            for g in range(GROUPS):
                lo = GROUPS + g * GROUP_EXPERTS
                pool.tensor_copy(router[:, :, lo:lo + GROUP_EXPERTS],
                                 r2_sb[:, g, :, :].rearrange("p i (c e) -> p (i c) e", c=2)).then_inc(router_ready, 1)
            pool.wait_ge(padded, 1)
            pool.wait_ge(z_act, 2)
            source, dest, n = u_pad, sum_a, 0
            for stage, w in enumerate(POOL_WINDOWS):
                half = w // 2
                pool.tensor_tensor(dest[:, stage:, PAD:], source[:, stage:, PAD:],
                                   source[:, stage:, PAD - half:PAD + SEQ - half], ALU.add).then_inc(pool_step, 1)
                n += 1
                pool.wait_ge(pool_step, n)
                sums = dest[:, stage, PAD:]
                pool.tensor_scalar(sums[:, PAD:], sums[:, PAD:], 1.0 / w, None, ALU.mult).then_inc(pool_step, 1)
                pool.tensor_tensor(sums[:, 0:PAD], sums[:, 0:PAD], edge[:, stage, :], ALU.mult).then_inc(pool_step, 1)
                n += 2
                pool.wait_ge(pool_step, n)
                pool.tensor_tensor(sums, sums, u_pad[:, stage, PAD:], ALU.subtract).then_inc(pooled, 1)
                source, dest = dest, (sum_b if dest is sum_a else sum_a)

        @block.vector
        def _(dve):
            steps = [0]

            def done(ins):
                steps[0] += 1
                ins.then_inc(vec, 1)
                dve.wait_ge(vec, steps[0])

            done(dve.memset(eps[:, :], EPS))
            dve.memset(v_area[0:HEADS, C_EARLY + SEQ:C_EARLY + BIAS_ROW], MASKED).then_inc(bias_sb_ok, 1)

            def normalise(which, t, source, gains, dest, ready):
                c = norm_cols(which, t)
                dve.wait_ge(rooted, c + 1)
                done(dve.reciprocal(rstd[:, c:c + 1], root[:, c:c + 1]))
                dve.scalar_tensor_tensor(out=dest, in0=source, scalar=rstd[:, c:c + 1], in1=gains,
                                         op0=ALU.mult, op1=ALU.mult).then_inc(ready, 1)

            def turned_out(which, t, half, bank, dest):
                dve.wait_ge(turned_ps, 4 * which + 2 * t + half + 1)
                dve.tensor_copy(dest[:, 4 * half:4 * half + 4, t * P:(t + 1) * P],
                                psum[:, bank, :].rearrange("p (c s) -> p c s", c=4)).then_inc(turned_vec, 1)

            dve.wait_ge(gain_in, 16)
            dve.wait_ge(x_in[0], 16)
            dve.wait_ge(x_in[1], 16)
            for t in range(TILES):
                normalise(0, t, x_sb[:, t, :], gain[:, :], h_sb[:, t, :], normed)
            dve.wait_ge(bias_ps, 1)
            dve.tensor_copy(v_area[0:HEADS, C_EARLY:C_EARLY + SEQ], psum[0:HEADS, 7, 0:SEQ]).then_inc(bias_sb_ok, 1)
            for t in range(TILES):
                turned_out(0, t, 1, 2 * t + 1, hT)
            for b in range(4):
                dve.wait_ge(flipped_ps, b + 1)
                dve.tensor_copy(bias_of[:, 2 * b:2 * b + 2, :], psum[:, b, :].rearrange("p (h k) -> p h k", h=2)
                                ).then_inc(bias_ready, 1)
            for b in range(2):
                dve.wait_ge(z_ps, 2 * b + 3)
                dve.tensor_scalar(qT[:, 2 * b:2 * b + 2, :], psum[:, b, :].rearrange("p (c t) -> p c t", c=2),
                                  HEAD_DIM ** -0.5, None, ALU.mult).then_inc(z_vec, 1)
            dve.wait_ge(z_ps, 7)
            dve.tensor_copy(v_sb[:, 0, :], psum[:, 6, :]).then_inc(z_vec, 1)
            dve.wait_ge(bias_ready, 4)
            dve.wait_ge(small_in, 32)
            for h in range(HEADS):
                dve.wait_ge(scores_ps, h + 1)
                if h >= 2:
                    dve.wait_ge(exped, 2 * (h - 1))
                for t in range(TILES):
                    lo, hi = (0, 128) if t == 0 else (128, 384)
                    ins = dve.tensor_tensor_reduce(scores[h % 2][:, lo:hi], psum[:, 4 + h % 2, lo:hi],
                                                   bias_of[:, h, 256 - (hi - lo):256], 1.0, 3 * MASKED, ALU.add,
                                                   ALU.max, row_max[:, h, t:t + 1])
                    done(ins)
                dve.tensor_scalar(neg_max[:, h, :], row_max[:, h, :], -1.0, None, ALU.mult).then_inc(scored, 1)
                if h == 2:
                    for g in range(POOL_GROUPS):
                        dve.wait_ge(pool_ps, 2 * (g // 2) + 2)
                        dve.tensor_scalar(mixT[:, 4 + g, :], psum[:, g // 2, 256 * (g % 2):256 * (g % 2) + 256],
                                          pool_scale[:, g:g + 1], None, ALU.mult).then_inc(pool_done, 1)
                if h % 4 == 3:
                    hh = 4 * (h // 4)
                    dve.wait_ge(exped, 2 * (h + 1))
                    done(dve.reciprocal(row_inv[:, :, hh:hh + 4], row_sum[:, :, hh:hh + 4]))
                    dve.wait_ge(attn_ps, h + 1)
                    dve.tensor_tensor(
                        h_sb[:, :, hh * HEAD_DIM:(hh + 4) * HEAD_DIM].rearrange("p t (h d) -> p t h d", h=4),
                        psum[:, 7, :].rearrange("p (t h d) -> p t h d", t=TILES, h=4),
                        row_inv[:, :, hh:hh + 4].unsqueeze(3).broadcast_to([P, TILES, 4, HEAD_DIM]),
                        ALU.mult).then_inc(attn_sb, 1)
            for t in range(TILES):
                dve.wait_ge(mix_ps, t + 1)
                if t == 0:
                    dve.wait_ge(attnT_ps, 2)
                dve.tensor_tensor(h_sb[:, t, :].rearrange("p (b n) -> p b n", b=2),
                                  x_sb[:, t, :].rearrange("p (b n) -> p b n", b=2),
                                  psum[:, 2 * t:2 * t + 2, :], ALU.add).then_inc(summed, 1)
            dve.wait_ge(summed, 2)
            dve.wait_ge(gain_in, 32)
            for t in range(TILES):
                normalise(1, t, h_sb[:, t, :], gain[:, :], h_sb[:, t, :], normed)
            for t in range(TILES):
                turned_out(1, t, 1, 5 + 2 * t, hT)

            def row(i):
                return small[:, i, :, :]

            def spread(v, n):
                return v.unsqueeze(2).broadcast_to([P, TILES, n])

            logits = ranks
            group_logits = small[:, 0, :, 0:GROUPS]
            dve.wait_ge(logits_ps, 2)
            dve.wait_ge(route_in, 16 * (3 + GROUPS))
            both = psum[:, 4, 0:128].rearrange("p (t n) -> p t n", t=TILES)
            dve.tensor_tensor(group_logits, both[:, :, 0:GROUPS],
                              router_bias[:, 0:GROUPS].unsqueeze(1).broadcast_to([P, TILES, GROUPS]),
                              ALU.add).then_inc(vec, 1)
            steps[0] += 1
            done(dve.tensor_tensor(logits[:, :, :], both[:, :, GROUPS:GROUPS + EXPERTS],
                                   router_bias[:, GROUPS:].unsqueeze(1).broadcast_to([P, TILES, EXPERTS]), ALU.add))

            def one_hot(values, n, top, dest, scratch):
                done(dve.tensor_reduce(top, values, AX, ALU.max))
                done(dve.tensor_tensor(dest, values, spread(top, n), ALU.is_equal))
                done(dve.tensor_tensor(dest, dest, first[:, 0:n].unsqueeze(1).broadcast_to([P, TILES, n]), ALU.mult))
                done(dve.tensor_reduce(scratch, dest, AX, ALU.max))
                done(dve.tensor_tensor(dest, dest, spread(scratch, n), ALU.is_equal))

            top_g, top_1, top_2, scratch = (tiny[:, i, :] for i in range(4))
            in_group = small[:, 3, :, 0:GROUPS]
            one_hot(group_logits, GROUPS, top_g, in_group, scratch)
            dve.tensor_tensor(small[:, 1, :, 0:GROUPS], group_logits, spread(top_g, GROUPS),
                              ALU.subtract).then_inc(exp_in, 1)
            done(dve.tensor_scalar(small[:, 4, :, 0:GROUPS], in_group, -1.0, -MASKED, ALU.add, ALU.mult))
            kept = row(5)
            done(dve.tensor_tensor(kept.rearrange("p t (g e) -> p t g e", g=GROUPS),
                                   logits[:, :, :].rearrange("p t (g e) -> p t g e", g=GROUPS),
                                   small[:, 4, :, 0:GROUPS].unsqueeze(3).broadcast_to([P, TILES, GROUPS, GROUP_EXPERTS]),
                                   ALU.add))
            best, second = row(6), row(7)
            one_hot(kept, EXPERTS, top_1, best, scratch)
            done(dve.scalar_tensor_tensor(out=kept, in0=best, scalar=MASKED, in1=kept, op0=ALU.mult, op1=ALU.add))
            one_hot(kept, EXPERTS, top_2, second, scratch)
            dve.tensor_tensor(tiny[:, 5, :], top_2, top_1, ALU.subtract).then_inc(exp_in, 1)
            taken = row(8)
            dve.tensor_tensor(taken, best, second, ALU.add).then_inc(chosen, 1)
            dve.wait_ge(exp_out, 1)
            done(dve.tensor_reduce(tiny[:, 7, :], small[:, 2, :, 0:GROUPS], AX, ALU.add))
            done(dve.reciprocal(tiny[:, 8, :], tiny[:, 7, :]))
            dve.wait_ge(exp_out, 2)
            done(dve.tensor_scalar(tiny[:, 9, :], tiny[:, 6, :], 1.0, None, ALU.add))
            done(dve.reciprocal(tiny[:, 10, :], tiny[:, 9, :]))
            done(dve.tensor_tensor(tiny[:, 11, :], tiny[:, 10, :], tiny[:, 8, :], ALU.mult))
            done(dve.tensor_tensor(tiny[:, 12, :], tiny[:, 11, :], tiny[:, 6, :], ALU.mult))
            gates = row(9)
            done(dve.tensor_tensor(gates, best, spread(tiny[:, 11, :], EXPERTS), ALU.mult))
            done(dve.tensor_tensor(row(10), second, spread(tiny[:, 12, :], EXPERTS), ALU.mult))
            done(dve.tensor_tensor(gates, gates, row(10), ALU.add))
            dve.wait_ge(chosen, 1)
            done(dve.tensor_scalar(row(11), taken, -NO_SLOT, NO_SLOT, ALU.mult, ALU.add))
            dve.wait_ge(rank_ps, 1)
            done(dve.tensor_tensor(ranks[:, :, :], psum[:, 5, 0:64].rearrange("p (t e) -> p t e", t=TILES),
                                   row(11), ALU.add))
            done(dve.tensor_reduce(most[:, :], psum[:, 5, 64:96], AX, ALU.max))
            dve.tensor_copy(most_int[:, :], most[:, :]).then_inc(routed, 1)

            def moe_step(step, quad0, s, moved_on=None):
                if moved_on is not None:
                    dve.wait_ge(next_ranks, moved_on)
                for q in range(QUADS_PER_STEP):
                    n = step * QUADS_PER_STEP + q
                    e0 = (quad0 + q) * QUAD

                    def of_quad(v):
                        return v[:, :, bass.ds(e0, QUAD)].unsqueeze(3).broadcast_to([P, TILES, QUAD, SLOTS])

                    dve.tensor_tensor(select, of_quad(ranks[:, :, :]),
                                      slot_no.unsqueeze(1).unsqueeze(1).broadcast_to([P, TILES, QUAD, SLOTS]),
                                      ALU.is_equal).then_inc(s["sel_step"], 1)
                    dve.wait_ge(s["sel_step"], n + 1)
                    dve.tensor_tensor(weighted, select, of_quad(gates), ALU.mult).then_inc(s["sel_ready"], 1)
                    dve.wait_ge(s["gath_ps"], n * 2 + 2)
                    dve.tensor_copy(xT[:, 4:8, :], psum[:, 7, :].rearrange("p (c s) -> p c s", c=4)
                                    ).then_inc(s["xT_vec"], 1)
                    dve.wait_ge(s["scat_ps"], n + 1)
                    dve.tensor_copy(scatterT, psum[:, 5, 0:256]).then_inc(s["scat_sb"], 1)
                    dve.wait_ge(s["silu_ready"], n + 1)
                    dve.wait_ge(s["up_ps"], n + 1)
                    dve.tensor_tensor(hidden, silu, psum[:, 5, :], ALU.mult).then_inc(s["hid_ready"], 1)
                    dve.wait_ge(s["down_ps"], n + 1)
                    dve.tensor_copy(down_sb[:, 512:1024], psum[:, 7, :]).then_inc(s["down_vec"], 1)

            dve.wait_ge(routed, 1)
            with dve.Fori(0, STEPS) as step:
                moe_step(step, step * QUADS_PER_STEP, main_s)
            with dve.If(dve.value_load(most_int[0:1, 0:1], min_val=0, max_val=SEQ) > SLOTS):
                with dve.Fori(0, PASSES - 1) as again:
                    dve.tensor_scalar(ranks[:, :, :], ranks[:, :, :], float(-SLOTS), None, ALU.add
                                      ).then_inc(next_ranks, 1)
                    with dve.Fori(0, STEPS) as step:
                        moe_step(again * STEPS + step, step * QUADS_PER_STEP, more_s, again + 1)
                dve.nop()

            dve.wait_ge(added, 1)
            for t in range(TILES):
                dve.tensor_tensor(x_sb[:, t, :].rearrange("p (b n) -> p b n", b=2),
                                  x_sb[:, t, :].rearrange("p (b n) -> p b n", b=2),
                                  psum[:, 2 * t:2 * t + 2, :], ALU.add).then_inc(summed, 1)
            dve.wait_ge(summed, 4)
            dve.wait_ge(tail_in, 32)
            for t in range(TILES):
                normalise(2, t, x_sb[:, t, :], g_ple, h_sb[:, t, :], normed)
            for t in range(TILES):
                turned_out(2, t, 1, 2 * t + 1, hT)
            for t in range(TILES):
                dve.wait_ge(opened, t + 1)
                dve.wait_ge(ple_sb, t + 1)
                done(dve.tensor_tensor(h_sb[:, t, :], h_sb[:, t, :], ple[:, t, :], ALU.mult))
                dve.tensor_tensor(x_sb[:, t, :], x_sb[:, t, :], h_sb[:, t, :], ALU.add).then_inc(final_x, 1)
            dve.wait_ge(final_x, 2)
            for t in range(TILES):
                normalise(3, t, x_sb[:, t, :], g_final, h_sb[:, t, :], final_out)

        @block.tensor
        def _(pe):
            def turn(which, t, banks, columns):
                pe.wait_ge(normed, 2 * which + t + 1)
                for c in range(8):
                    last = pe.transpose(psum[:, banks[c // 4], P * (c % 4):P * (c % 4) + P], columns(t, c), ident)
                    if which == 1 and t == 0 and c < W_OUT_UNITS:
                        last.then_inc(ring_free, 1)
                    if c % 4 == 3:
                        last.then_inc(turned_ps, 1)

            def pairs(t, c):
                i, c2 = divmod(c, 2)
                return h_sb[:, t, 256 * i + c2:256 * i + 256:2]

            def plain(t, c):
                return h_sb[:, t, P * c:P * c + P]

            pe.wait_ge(consts_in, 16)
            pe.wait_ge(early_in, 32)
            pe.matmul(psum[0:HEADS, 7, 0:SEQ], rel_bias[:, :], bucket_of, start=True, stop=True).then_inc(bias_ps, 1)
            for t in range(TILES):
                turn(0, t, (2 * t, 2 * t + 1), pairs)
            pe.wait_ge(bias_in, 16)
            pe.wait_ge(turned_act, 2)
            pe.wait_ge(turned_vec, 2)
            for h in range(HEADS):
                last = pe.matmul(psum[:, h // 2, SEQ * (h % 2):SEQ * (h % 2) + SEQ], flip, flipped[:, h, :],
                                 start=True, stop=True)
                if h % 2:
                    last.then_inc(flipped_ps, 1)

            pe.wait_ge(bias_sb_ok, 2)
            pe.wait_ge(bias_ready, 4)
            chunk_bank = {**{c: c // 2 for c in range(8)}, **{12 + g: 4 + g // 2 for g in range(4)}}
            order = [12, 13, 14, 15, 0, 1, 4, 5, 2, 3, 6, 7]
            w = [unit(i).rearrange("p (c n) -> p c n", c=2) for i in range(W_IN_UNITS)]

            def project(c, m):
                half = SEQ * (m % 2)
                return pe.matmul(psum[:, chunk_bank[m], half:half + SEQ], w[c // 2][:, c % 2, P * m:P * m + P],
                                 hT[:, c, :], start=(c == 0 and m % 2 == 0), stop=(c == 7), skip_group_check=True)

            def project_v(c, t):
                return pe.matmul(psum[:, 6 + t, :], hT[:, c, t * P:(t + 1) * P], w[c // 2][:, c % 2, 1024:1536],
                                 start=(c == 0), stop=(c == 7), skip_group_check=True)

            for c in range(6):
                if c % 2 == 0:
                    pe.wait_ge(slot_in[c // 2], 16)
                for m in order:
                    project(c, m)
                for t in range(TILES):
                    last = project_v(c, t)
                if c % 2:
                    last.then_inc(ring_free, 1)
            pe.wait_ge(slot_in[3], 16)
            for i in range(0, 12, 2):
                for m in order[i:i + 2]:
                    for c in (6, 7):
                        last = project(c, m)
                last.then_inc(z_ps, 1)
            for t in range(TILES):
                for c in (6, 7):
                    last = project_v(c, t)
                last.then_inc(z_ps, 1)

            def score(h):
                r = HEAD_DIM * (h % 2)
                q_h, k_h = (v[r:r + HEAD_DIM, h // 2, :] for v in (qT, kT))
                if h >= 2:
                    pe.wait_ge(scored, h - 1)
                last = pe.matmul(psum[:, 4 + h % 2, 0:128], q_h[:, 0:P], k_h[:, 0:P], start=True, stop=True)
                if h == 0:
                    last.then_inc(ring_free, 1)
                pe.matmul(psum[:, 4 + h % 2, 128:384], q_h[:, P:], k_h, start=True, stop=True).then_inc(scores_ps, 1)

            def mix(c, t, first_one, last_one):
                w_c = unit(W_IN_UNITS + c // 4).rearrange("p (c n) -> p c n", c=4)[:, c % 4, :]
                for half in range(2):
                    last = pe.matmul(psum[:, 2 * t + half, :], mixT[:, c, t * P:(t + 1) * P],
                                     w_c[:, 512 * half:512 * half + 512], start=first_one, stop=last_one,
                                     skip_group_check=True)
                return last

            pe.wait_ge(z_vec, 2)
            pe.wait_ge(z_act, 4)
            score(0)
            score(1)
            pe.wait_ge(z_vec, 3)
            pe.wait_ge(z_act, 5)
            for h in range(HEADS):
                pe.wait_ge(exped, 2 * (h + 1))
                if h >= 1:
                    pe.wait_ge(probs_sb, h)
                if h == 4:
                    pe.wait_ge(attnT_sb, 1)
                for i in range(3):
                    last = pe.transpose(psum[:, 6, P * i:P * i + P], probs[h % 2][:, P * i:P * i + P], ident)
                last.then_inc(probs_ps, 1)
                if h + 2 < HEADS:
                    score(h + 2)
                if h == 2:
                    pe.wait_ge(small_in, 32)
                    for g in range(POOL_GROUPS):
                        pe.wait_ge(pooled, g + 1)
                        means = (sum_a, sum_b)[g % 2]
                        pe.matmul(psum[:, g // 2, 256 * (g % 2):256 * (g % 2) + 256], w_pool[:, g, :],
                                  means[:, g, PAD:], start=True, stop=True).then_inc(pool_ps, 1)
                if 4 <= h:
                    if h == 4:
                        pe.wait_ge(pool_done, POOL_GROUPS)
                        pe.wait_ge(slot_in[5], 16)
                    for t in range(TILES):
                        mix(h, t, h == 4, False)
                pe.wait_ge(probs_sb, h + 1)
                if h == 4:
                    pe.wait_ge(attn_sb, 1)
                o = psum[:, 7, :].rearrange("p (t h d) -> p t h d", t=TILES, h=4)
                values = v_sb[:, :, h * HEAD_DIM:(h + 1) * HEAD_DIM]
                pe.matmul(o[:, 0, h % 4, :], probsT[h % 2][:, 0:P], values[:, 0, :], start=True, stop=True)
                pe.matmul(o[:, 1, h % 4, :], probsT[h % 2][:, P:2 * P], values[:, 0, :], start=True, stop=False)
                pe.matmul(o[:, 1, h % 4, :], probsT[h % 2][:, 2 * P:], values[:, 1, :], start=False, stop=True
                          ).then_inc(attn_ps, 1)
                if h % 4 == 3:
                    pe.wait_ge(attn_sb, h // 4 + 1)
                    for c in range(2):
                        for t in range(TILES):
                            lo = (2 * (h // 4) + c) * P
                            last = pe.transpose(psum[:, 6, SEQ * c + P * t:SEQ * c + P * t + P],
                                                h_sb[:, t, lo:lo + P], ident)
                    last.then_inc(attnT_ps, 1)
            pe.wait_ge(slot_in[4], 16)
            pe.wait_ge(attnT_sb, 2)
            for t in range(TILES):
                for c in range(4):
                    last = mix(c, t, False, c == 3)
                last.then_inc(mix_ps, 1)

            for t in range(TILES):
                turn(1, t, (4 + 2 * t, 5 + 2 * t), pairs)
            pe.wait_ge(router_ready, 1 + GROUPS)
            pe.wait_ge(turned_act, 4)
            pe.wait_ge(turned_vec, 4)
            for t in range(TILES):
                for c in range(8):
                    last = pe.matmul(psum[:, 4, 64 * t:64 * t + GROUPS + EXPERTS], hT[:, c, t * P:(t + 1) * P],
                                     router[:, c, :], start=(c == 0), stop=(c == 7))
                last.then_inc(logits_ps, 1)
            pe.wait_ge(chosen, 1)
            taken = small[:, 8, :, :]
            pe.matmul(psum[:, 5, 0:32], earlier, taken[:, 0, :], start=True, stop=True)
            pe.matmul(psum[:, 5, 32:64], earlier, taken[:, 1, :], start=True, stop=False)
            pe.matmul(psum[:, 5, 32:64], ones, taken[:, 0, :], start=False, stop=True)
            pe.matmul(psum[:, 5, 64:96], ones, taken[:, 0, :], start=True, stop=False)
            pe.matmul(psum[:, 5, 64:96], ones, taken[:, 1, :], start=False, stop=True).then_inc(rank_ps, 1)

            def moe_step(step, s, arrived, free, earlier_uses):
                def unit_in(u):
                    slot = (FIRST_EXPERT_UNIT + u) % RING
                    pe.wait_ge(arrived[slot], step * (16 * STEP_USES) + 16 * (earlier_uses[slot] + u // RING + 1))
                    return expert_unit(slot)

                def strips(bank, lhsT, w_u, lo, start, stop, used_before):
                    for e in range(QUAD):
                        last = pe.matmul(psum[SLOTS * e:SLOTS * e + SLOTS, bank, :],
                                         lhsT[:, SLOTS * e:SLOTS * e + SLOTS], w_u[:, e, lo:lo + 512],
                                         start=start, stop=stop, skip_group_check=True)
                        if used_before and e == 0:
                            last.then_inc(free, 1)
                    return last

                for q in range(QUADS_PER_STEP):
                    n = step * QUADS_PER_STEP + q
                    pe.wait_ge(s["sel_ready"], n + 1)
                    for c in range(8):
                        for t in range(TILES):
                            last = pe.matmul(psum[:, 6 + c // 4, P * (c % 4):P * (c % 4) + P], pairs(t, c),
                                             select[:, t, :, :], start=(t == 0), stop=(t == 1))
                        if c % 4 == 3:
                            last.then_inc(s["gath_ps"], 1)
                    for t in range(TILES):
                        last = pe.matmul(psum[:, 5, P * t:P * t + P], weighted[:, t, :, :], ident,
                                         start=True, stop=True)
                    last.then_inc(s["scat_ps"], 1)
                    pe.wait_ge(s["xT_act"], n + 1)
                    pe.wait_ge(s["xT_vec"], n + 1)
                    for kind, name in enumerate(("gate_ps", "up_ps")):
                        if kind == 1:
                            pe.wait_ge(s["scat_sb"], n + 1)
                        for i in range(4):
                            w_u = unit_in(q * QUAD_UNITS + 4 * kind + i)
                            for c2 in range(2):
                                last = strips(4 + kind, xT[:, 2 * i + c2, :], w_u, 512 * c2, i + c2 == 0,
                                              i == 3 and c2 == 1, c2 == 0 and (kind, i) != (0, 0))
                        last.then_inc(s[name], 1)
                    pe.wait_ge(s["hid_ready"], n + 1)
                    for c in range(4):
                        last = pe.transpose(psum[:, 4, P * c:P * c + P], hidden[:, P * c:P * c + P], ident)
                        if c == 0:
                            last.then_inc(free, 1)
                    last.then_inc(s["hidT_ps"], 1)
                    pe.wait_ge(s["hidT_sb"], n + 1)
                    for i in range(4):
                        w_u = unit_in(q * QUAD_UNITS + 8 + i)
                        for half in range(2):
                            last = strips(6 + half, hiddenT[:, i, :], w_u, 512 * half, i == 0, i == 3,
                                          half == 0 and i > 0)
                    last.then_inc(s["down_ps"], 1)
                    pe.wait_ge(s["down_act"], n + 1)
                    pe.wait_ge(s["down_vec"], n + 1)
                    for t in range(TILES):
                        for half in range(2):
                            last = pe.matmul(psum[:, 2 * t + half, :], scatterT[:, t * P:(t + 1) * P],
                                             down_sb[:, 512 * half:512 * half + 512], start=False, stop=False,
                                             skip_group_check=True)
                            if t + half == 0:
                                last.then_inc(free, 1)

            with pe.Fori(0, STEPS) as step:
                moe_step(step, main_s, slot_in, ring_free, [int(i < FIRST_EXPERT_UNIT) for i in range(RING)])
            pe.wait_ge(routed, 1)
            with pe.If(pe.value_load(most_int[0:1, 0:1], min_val=0, max_val=SEQ) > SLOTS):
                with pe.Fori(0, PASSES - 1) as again:
                    with pe.Fori(0, STEPS) as step:
                        moe_step(again * STEPS + step, more_s, more_in, more_free, [0] * RING)
                pe.nop()

            pe.wait_ge(p_in, 16)
            for t in range(TILES):
                for c in range(2):
                    last = pe.transpose(psum[:, 4, SEQ * c + P * t:SEQ * c + P * t + P],
                                        p_sb[:, t, c * P:(c + 1) * P], ident)
                    if t + c == 0:
                        last.then_inc(added, 1)
            last.then_inc(pT_ps, 1)
            tail_unit = FIRST_EXPERT_UNIT + EXPERT_UNITS

            def tail_in_slot(i):
                slot, uses = (tail_unit + i) % RING, (tail_unit + i) // RING + 1
                pe.wait_ge(slot_in[slot], 16 * uses)
                return unit(slot)

            pe.wait_ge(pT_sb, 1)
            w_p = tail_in_slot(2)[:, 0:2048].rearrange("p (c n) -> p c n", c=2)
            for t in range(TILES):
                for half in range(2):
                    for c in range(2):
                        last = pe.matmul(psum[:, 4 + 2 * t + half, :], pT[:, c, t * P:(t + 1) * P],
                                         w_p[:, c, 512 * half:512 * half + 512], start=(c == 0), stop=(c == 1))
                last.then_inc(ple_ps, 1)
            for t in range(TILES):
                turn(2, t, (2 * t, 2 * t + 1), plain)
            w_g = [tail_in_slot(i).rearrange("p (c n) -> p c n", c=4) for i in range(2)]
            for t in range(TILES):
                pe.wait_ge(turned_act, 5 + t)
                pe.wait_ge(turned_vec, 5 + t)
                pe.wait_ge(ple_sb, t + 1)
                for half in range(2):
                    for c in range(8):
                        last = pe.matmul(psum[:, 4 + 2 * t + half, :], hT[:, c, t * P:(t + 1) * P],
                                         w_g[c // 4][:, c % 4, 512 * half:512 * half + 512],
                                         start=(c == 0), stop=(c == 7))
                last.then_inc(open_ps, 1)


def constant_table():
    import math
    table = np.zeros((P, C_KEPT + C_EARLY), np.float32)
    table[:, C_IDENT:C_IDENT + P] = np.eye(P)
    table[:, C_EARLIER:C_EARLIER + P] = np.triu(np.ones((P, P)), 1)
    table[:, C_ONES:C_ONES + P] = 1.0
    table[:, C_SLOT:C_SLOT + SLOTS] = np.arange(SLOTS)
    table[:, C_FIRST:C_FIRST + EXPERTS] = EXPERTS - np.arange(EXPERTS)
    for g, w in enumerate(POOL_WINDOWS):
        table[:, C_EDGE + PAD * g:C_EDGE + PAD * (g + 1)] = 1.0 / np.minimum(np.arange(PAD) + 1, w)
    table[:, C_KEPT + C_FLIP:C_KEPT + C_FLIP + P] = np.eye(P)[::-1]
    distance = SEQ - 1 - np.arange(SEQ)
    exact = BUCKETS // 2
    far = np.log(np.maximum(distance, 1).astype(np.float32) / np.float32(exact))
    far = far / np.float32(math.log(MAX_DIST / exact)) * np.float32(BUCKETS - exact)
    bucket = np.where(distance < exact, distance, np.minimum(exact + far.astype(np.int32), BUCKETS - 1))
    table[bucket, C_KEPT + C_BUCKET + np.arange(SEQ)] = 1.0
    return table


INPUTS = ["x", "p", "g_mix", "w_in", "w_pool", "pool_scale", "w_out", "rel_bias", "g_ffn", "w_r1", "b_r1", "w_r2",
          "b_r2", "w_gate", "w_up", "w_down", "g_ple", "w_ple_proj", "w_ple_gate", "g_final"]


def kernel(**inputs):
    import concourse.bacc as bacc
    from concourse.bass_utils import run_bass_kernel_spmd

    nc = bacc.Bacc("TRN2", target_bir_lowering=False, num_devices=1)
    arrays, aps = {}, {}
    for name in [*INPUTS, "consts"]:
        array = constant_table() if name == "consts" else np.ascontiguousarray(inputs[name])
        arrays[f"in_{name}"] = array
        aps[name] = nc.dram_tensor(f"in_{name}", array.shape, mybir.dt.from_np(array.dtype), kind="ExternalInput").ap()
    out = nc.dram_tensor("out_x", (1, SEQ, D), F32, kind="ExternalOutput").ap()
    layer_kernel(nc, aps, out)
    result = run_bass_kernel_spmd(nc, [arrays], core_ids=[0])
    return result.results[0]["out_x"]
```

```python
from contextlib import ExitStack

import numpy as np

import concourse.bass as bass
from concourse import mybir

F32 = mybir.dt.float32
I32 = mybir.dt.int32
ALU = mybir.AluOpType
ACT = mybir.ActivationFunctionType
AX = mybir.AxisListType.X

P = 128
SEQ = 256
TILES = SEQ // P
D = 1024
HEADS, HEAD_DIM = 8, 64
D_ATTN = HEADS * HEAD_DIM
GROUPS, GROUP_EXPERTS, D_EXPERT = 4, 8, 512
EXPERTS = GROUPS * GROUP_EXPERTS
QUAD = 4
SLOTS = 32
QUADS_PER_STEP = 2
STEPS = EXPERTS // QUAD // QUADS_PER_STEP
PASSES = SEQ // SLOTS
D_PLE = 256
POOL_WINDOWS = (2, 4, 8, 16)
POOL_GROUPS = len(POOL_WINDOWS)
PAD = 16
BUCKETS, MAX_DIST = 32, 128
EPS = 1e-6
MASKED = -1e30
RING = 8
UNIT = 4096
W_IN_UNITS, W_OUT_UNITS, QUAD_UNITS = 4, 2, 12
FIRST_EXPERT_UNIT = W_IN_UNITS + W_OUT_UNITS
STEP_UNITS = QUADS_PER_STEP * QUAD_UNITS
STEP_USES = STEP_UNITS // RING
EXPERT_UNITS = STEPS * STEP_UNITS
BIAS_ROW = 384
NO_SLOT = 1000.0

C_IDENT, C_FLIP, C_EARLIER, C_ONES, C_SLOT, C_FIRST, C_EDGE = 0, 128, 256, 384, 512, 544, 576
C_KEPT = C_EDGE + POOL_GROUPS * PAD


def layer_kernel(nc, a, out):
    with ExitStack() as ctx:
        def sbuf(name, cols, dt=F32, rows=P):
            return ctx.enter_context(nc.sbuf_tensor(name, [rows, cols], dt))

        def sem(name):
            return ctx.enter_context(nc.semaphore(name))

        ring = ctx.enter_context(nc.sbuf_tensor("ring", [P, RING, UNIT], F32))
        x_sb = ctx.enter_context(nc.sbuf_tensor("x_sb", [P, TILES, D], F32))
        h_sb = ctx.enter_context(nc.sbuf_tensor("h_sb", [P, TILES, D], F32))
        hT = ctx.enter_context(nc.sbuf_tensor("hT", [P, 8, SEQ], F32))
        qk_area = sbuf("qk_area", 2048)
        v_area = sbuf("v_area", 1024)
        bias_area = sbuf("bias_area", 2048)
        pool_area = sbuf("pool_area", 3 * POOL_GROUPS * (SEQ + PAD))
        attn_area = sbuf("attn_area", 2304)
        gain = sbuf("gain", D)
        consts = sbuf("consts", C_KEPT)
        w_pool = ctx.enter_context(nc.sbuf_tensor("w_pool_sb", [P, POOL_GROUPS, P], F32))
        pool_scale = sbuf("pool_scale_sb", POOL_GROUPS)
        router = ctx.enter_context(nc.sbuf_tensor("router", [P, 8, GROUPS + EXPERTS], F32))
        router_bias = sbuf("router_bias", 1, rows=GROUPS + EXPERTS)
        rel_bias = sbuf("rel_bias_sb", HEADS, rows=BUCKETS)
        eps = sbuf("eps", 1)
        warm = sbuf("warm", 16)
        sum_sq = sbuf("sum_sq", 16)
        base = sbuf("base", 8)
        root = sbuf("root", 8)
        rstd = sbuf("rstd", 8)
        row_max = ctx.enter_context(nc.sbuf_tensor("row_max", [P, HEADS, TILES], F32))
        neg_max = ctx.enter_context(nc.sbuf_tensor("neg_max", [P, HEADS, TILES], F32))
        row_sum = ctx.enter_context(nc.sbuf_tensor("row_sum", [P, TILES, HEADS], F32))
        row_inv = ctx.enter_context(nc.sbuf_tensor("row_inv", [P, TILES, HEADS], F32))
        routing = sbuf("routing", 12 * TILES * EXPERTS)
        tiny = ctx.enter_context(nc.sbuf_tensor("tiny", [P, 16, TILES], F32))
        ranks = ctx.enter_context(nc.sbuf_tensor("ranks", [P, TILES, EXPERTS], F32))
        most = sbuf("most", 1)
        most_int = sbuf("most_int", 1, I32)

        ident = consts[:, C_IDENT:C_IDENT + P]
        flip = consts[:, C_FLIP:C_FLIP + P]
        earlier = consts[:, C_EARLIER:C_EARLIER + P]
        ones = consts[:, C_ONES:C_ONES + P]
        slot_no = consts[:, C_SLOT:C_SLOT + SLOTS]
        first = consts[:, C_FIRST:C_FIRST + EXPERTS]
        edge = consts[:, C_EDGE:C_KEPT].rearrange("p (g t) -> p g t", g=POOL_GROUPS)

        small = routing[:, :].rearrange("p (i t e) -> p i t e", i=12, t=TILES)
        r1_sb = routing[:, 0:32].rearrange("p (i c g) -> p i c g", i=4, c=2)
        r2_sb = routing[:, 32:288].rearrange("p (g i c) -> p g i c", g=GROUPS, i=4)
        logits = routing[:, 0:128].rearrange("p (t n) -> p t n", t=TILES)
        shifted, shifted_exp, in_group, penalty = (
            routing[:, 128 + 8 * i:136 + 8 * i].rearrange("p (t n) -> p t n", t=TILES) for i in range(4))
        logitsT = routing[0:GROUPS + EXPERTS, 512:768]

        qT = qk_area[:, 0:1024].rearrange("p (c t) -> p c t", c=4)
        kT = qk_area[:, 1024:2048].rearrange("p (c t) -> p c t", c=4)
        w_ple_sb = qk_area[:, :].rearrange("p (c n) -> p c n", c=2)
        down_sb = qk_area[:, 0:1024]
        bucket_of = v_area[0:BUCKETS, 0:SEQ]
        bias_row = v_area[0:HEADS, SEQ:SEQ + BIAS_ROW]
        v_sb = v_area[:, :].rearrange("p (t n) -> p t n", t=TILES)
        ple = [v_area[:, :], hT[:, 0:4, :].rearrange("p c t -> p (c t)")]
        bias_of = bias_area[:, :].rearrange("p (h k) -> p h k", h=HEADS)
        xT = bias_area[:, 0:1024].rearrange("p (c s) -> p c s", c=8)
        hidden = bias_area[:, 1024:1536]
        hiddenT = bias_area[:, 1536:2048].rearrange("p (c s) -> p c s", c=4)
        width = POOL_GROUPS * (SEQ + PAD)
        u_pad, sum_a, sum_b = (pool_area[:, i * width:(i + 1) * width].rearrange("p (g t) -> p g t", g=POOL_GROUPS)
                               for i in range(3))
        select = pool_area[:, 0:256].rearrange("p (t e s) -> p t e s", t=TILES, e=QUAD)
        weighted = pool_area[:, 256:512].rearrange("p (t e s) -> p t e s", t=TILES, e=QUAD)
        scatterT = pool_area[:, 512:768]
        g_ple = pool_area[:, 768:1792]
        g_final = pool_area[:, 1792:2816]
        scores = [attn_area[:, 384 * i:384 * i + 384] for i in range(2)]
        probs = [attn_area[:, 768 + 384 * i:768 + 384 * i + 384] for i in range(2)]
        probsT = [attn_area[:, 1536 + 384 * i:1536 + 384 * i + 384] for i in range(2)]
        silu = attn_area[:, 0:512]
        scratch = attn_area[:, 0:1024]
        pT = attn_area[:, 1536:2048].rearrange("p (c t) -> p c t", c=2)
        p_sb = h_sb[:, 0, 512:1024].rearrange("p (t n) -> p t n", t=TILES)
        gateT = bias_area[:, :].rearrange("p (c t) -> p c t", c=8)
        mixT = hT

        psum = ctx.enter_context(nc.psum_tensor("psum", [P, 8, 512], F32))

        bias_dram = nc.dram_tensor("bias_by_distance", [HEADS, BIAS_ROW], F32, kind="Internal").ap()

        x_in = [sem(f"x_in{t}") for t in range(TILES)]
        consts_in, early_in, gain_in, ffn_gain_in, small_in, route_in = map(
            sem, ("consts_in", "early_in", "gain_in", "ffn_gain_in", "small_in", "route_in"))
        bias_out, bias_in, tail_in, p_in, w_ple_in, out_done = map(
            sem, ("bias_out", "bias_in", "tail_in", "p_in", "w_ple_in", "out_done"))
        slot_in = [sem(f"slot_in{s}") for s in range(RING)]
        more_in = [sem(f"more_in{s}") for s in range(RING)]
        ring_free, more_free = sem("ring_free"), sem("more_free")
        vec = sem("vector_step")
        squared, based, rooted, normed, turned_ps, turned_act, turned_vec = map(
            sem, ("squared", "based", "rooted", "normed", "turned_ps", "turned_act", "turned_vec"))
        summed = sem("summed")
        bias_ps, bias_row_ready = map(sem, ("bias_ps", "bias_row_ready"))
        z_ps, z_act, z_vec = map(sem, ("z_ps", "z_act", "z_vec"))
        pooled, pool_step, pool_ps, pool_done, padded = map(
            sem, ("pooled", "pool_step", "pool_ps", "pool_done", "padded"))
        router_ready = sem("router_ready")
        scores_ps, scored, exped, probs_ps, probs_sb = map(
            sem, ("scores_ps", "scored", "exped", "probs_ps", "probs_sb"))
        attn_ps, attn_sb, attnT_ps, attnT_sb, mix_ps = map(
            sem, ("attn_ps", "attn_sb", "attnT_ps", "attnT_sb", "mix_ps"))
        logitsT_ps, logitsT_sb, logits_ps, exp_in, exp_out, chosen, rank_ps, routed = map(
            sem, ("logitsT_ps", "logitsT_sb", "logits_ps", "exp_in", "exp_out", "chosen", "rank_ps", "routed"))
        pT_ps, pT_sb, ple_ps, ple_sb = map(sem, ("pT_ps", "pT_sb", "ple_ps", "ple_sb"))
        open_ps, opened, final_x, final_out = map(
            sem, ("gate_logits_ps", "gate_opened", "final_x", "final_out"))

        names = ("selected", "sel_ready", "gath_ps", "xT_act", "xT_vec", "scat_ps", "scat_sb", "gate_ps", "silu_ready", "up_ps",
                 "hid_ready", "hidT_ps", "hidT_sb", "down_ps", "down_act", "down_vec", "scattered")
        main_s = {n: sem("m_" + n) for n in names}
        more_s = {n: sem("o_" + n) for n in names}
        next_ranks = sem("next_ranks")

        w_in = a["w_in"][0].rearrange("(i p c) n -> i p (c n)", i=W_IN_UNITS, c=2)
        w_out = a["w_out"][0].rearrange("(i c p) n -> i p c n", i=W_OUT_UNITS, c=4)
        w_ple_gate = a["w_ple_gate"][0].rearrange("(i c p) n -> i p c n", i=2, c=4)
        w_ple = a["w_ple_proj"][0].rearrange("(c p) n -> p c n", p=P)
        w_gate, w_up = (a[n][0].rearrange("g (q e) (i p c) f -> (g q) i p e (c f)", e=QUAD, p=P, c=2)
                        for n in ("w_gate", "w_up"))
        w_down = a["w_down"][0].rearrange("g (q e) (i p) n -> (g q) i p e n", e=QUAD, p=P)
        x_dram = a["x"][0].rearrange("(t p) n -> t p n", p=P)
        out_dram = out[0].rearrange("(t p) n -> t p n", p=P)
        p_dram = a["p"][0, 0].rearrange("(t p) n -> p t n", p=P)

        def broadcast(row):
            return row.rearrange("(o n) -> o n", o=1).broadcast_to([P, row.shape[0]])

        def unit(slot):
            return ring[:, slot, :]

        def expert_unit(slot):
            return unit(slot).rearrange("p (e n) -> p e n", e=QUAD)

        def half_of(v, t, half):
            return v[:, t, 512 * half:512 * half + 512]

        block = ctx.enter_context(nc.Block())

        @block.sync
        def _(sp):
            for t in range(TILES):
                sp.dma_start(x_sb[:, t, :], x_dram[t]).then_inc(x_in[t], 16)
            sp.dma_start(consts[:, :], a["consts"][:, 0:C_KEPT]).then_inc(consts_in, 16)
            sp.dma_start(gain[:, :], broadcast(a["g_mix"][0])).then_inc(gain_in, 16)
            sp.sem_inc(ring_free, RING)

            def load_w_in(i):
                sp.dma_start(unit(i), w_in[i]).then_inc(slot_in[i], 16)

            load_w_in(0)
            sp.dma_start(v_area[0:BUCKETS, 0:SEQ], a["consts"][0:BUCKETS, C_KEPT:]).then_inc(early_in, 16)
            sp.dma_start(rel_bias[:, :], a["rel_bias"]).then_inc(early_in, 16)
            for i in range(1, W_IN_UNITS):
                load_w_in(i)
            sp.dma_start(w_pool[:, :, :], a["w_pool"][0].rearrange("g c d -> c g d")).then_inc(small_in, 16)
            with nc.allow_non_contiguous_dma(reason="512 single values"):
                sp.dma_start(pool_scale[:, :], a["pool_scale"][0].rearrange("(g d) -> d g", d=P)).then_inc(small_in, 16)
                sp.dma_start(r1_sb, a["w_r1"][0].rearrange("(i p c) g -> p i c g", i=4, c=2)).then_inc(route_in, 16)
                for g in range(GROUPS):
                    sp.dma_start(r2_sb[:, g, :, :], a["w_r2"][0, g].rearrange("(i p c) e -> p i (c e)", i=4, c=2)
                                 ).then_inc(route_in, 16)
                sp.dma_start(router_bias[0:GROUPS, :], a["b_r1"][0].rearrange("(g o) -> g o", o=1)).then_inc(route_in, 16)
                sp.dma_start(router_bias[GROUPS:, :], a["b_r2"][0].rearrange("g (e o) -> (g e) o", o=1)
                             ).then_inc(route_in, 16)
            sp.wait_ge(bias_in, 16)
            for i in range(W_OUT_UNITS):
                s = W_IN_UNITS + i
                sp.dma_start(unit(s).rearrange("p (c n) -> p c n", c=4), w_out[i]).then_inc(slot_in[s], 16)

            def load_step(step, quad0, arrived, free, already):
                for u in range(STEP_UNITS):
                    q, i = divmod(u, QUAD_UNITS)
                    kind, part = divmod(i, 4)
                    w = (w_gate, w_up, w_down)[kind]
                    slot = (FIRST_EXPERT_UNIT + u) % RING
                    sp.wait_ge(free, step * STEP_UNITS + already + u + 1)
                    sp.dma_start(expert_unit(slot), w[bass.ds(quad0 + q, 1), part][0]).then_inc(arrived[slot], 16)

            with sp.Fori(0, STEPS) as step:
                load_step(step, step * QUADS_PER_STEP, slot_in, ring_free, FIRST_EXPERT_UNIT)

            sp.wait_ge(routed, 1)
            with sp.If(sp.value_load(most_int[0:1, 0:1], min_val=0, max_val=SEQ) > SLOTS):
                sp.wait_ge(ring_free, RING + FIRST_EXPERT_UNIT + EXPERT_UNITS)
                sp.sem_inc(more_free, RING)
                with sp.Fori(0, PASSES - 1) as again:
                    with sp.Fori(0, STEPS) as step:
                        load_step(again * STEPS + step, step * QUADS_PER_STEP, more_in, more_free, 0)
                sp.wait_ge(more_free, RING + (PASSES - 1) * EXPERT_UNITS)
            for i in range(2):
                n = FIRST_EXPERT_UNIT + EXPERT_UNITS + i
                sp.wait_ge(ring_free, n + 1)
                sp.dma_start(unit(n % RING).rearrange("p (c n) -> p c n", c=4), w_ple_gate[i]
                             ).then_inc(slot_in[n % RING], 16)
            for t in range(TILES):
                for half in range(2):
                    sp.wait_ge(final_out, 2 * t + half + 1)
                    sp.dma_start(out_dram[t][:, 512 * half:512 * half + 512], half_of(h_sb, t, half)
                                 ).then_inc(out_done, 16)
            sp.wait_ge(out_done, 16 * 2 * TILES)

        @block.scalar
        def _(act):
            warmed = [0]

            def load_table(func):
                i = warmed[0]
                warmed[0] += 1
                act.activation(warm[:, i:i + 1], eps[:, 0:1], func)

            def square(which, t, half, source, ready, at):
                act.wait_ge(ready, at)
                n = 4 * which + 2 * t + half
                if n:
                    act.wait_ge(squared, n)
                act.activation(scratch[:, 512 * half:512 * half + 512], source, ACT.Square,
                               accum_out=sum_sq[:, n:n + 1]).then_inc(squared, 1)

            def root_of(which, t):
                c = 2 * which + t
                act.wait_ge(squared, 2 * c + 2)
                act.wait_ge(based, c + 1)
                act.activation(root[:, c:c + 1], sum_sq[:, 2 * c + 1:2 * c + 2], ACT.Sqrt, scale=1.0 / D,
                               bias=base[:, c:c + 1]).then_inc(rooted, 1)

            def turned_out(which, t, bank, dest):
                act.wait_ge(turned_ps, 4 * which + 2 * t + 1)
                act.copy(dest[:, 0:4, t * P:(t + 1) * P],
                         psum[:, bank, :].rearrange("p (c s) -> p c s", c=4)).then_inc(turned_act, 1)

            act.wait_ge(vec, 1)
            load_table(ACT.Sqrt)
            for t in range(TILES):
                for half in range(2):
                    square(0, t, half, half_of(x_sb, t, half), x_in[t], 16)
                root_of(0, t)
            for t in range(TILES):
                turned_out(0, t, 2 * t, hT)
            load_table(ACT.Exp)

            for b in range(2):
                act.wait_ge(z_ps, b + 1)
                act.copy(u_pad[:, 2 * b:2 * b + 2, PAD:], psum[:, 4 + b, :].rearrange("p (c t) -> p c t", c=2)
                         ).then_inc(z_act, 1)
            for b in range(2):
                act.wait_ge(z_ps, 2 * b + 4)
                act.copy(kT[:, 2 * b:2 * b + 2, :], psum[:, 2 + b, :].rearrange("p (c t) -> p c t", c=2)
                         ).then_inc(z_act, 1)

            def exponents(h):
                act.wait_ge(scored, h + 1)
                if h >= 2:
                    act.wait_ge(probs_ps, h - 1)
                for t in range(TILES):
                    lo, hi = (0, 128) if t == 0 else (128, 384)
                    act.activation(probs[h % 2][:, lo:hi], scores[h % 2][:, lo:hi], ACT.Exp,
                                   bias=neg_max[:, h, t:t + 1], accum_out=row_sum[:, t, h:h + 1]).then_inc(exped, 1)

            def head_pair_out(pair):
                act.wait_ge(attnT_ps, pair + 1)
                act.copy(mixT[:, pair, :], psum[:, 7, 256:512]).then_inc(attnT_sb, 1)

            exponents(0)
            exponents(1)
            act.wait_ge(z_ps, 8)
            act.copy(v_sb[:, 1, :], psum[:, 7, :]).then_inc(z_act, 1)
            for h in range(HEADS):
                if 2 <= h + 1 < HEADS:
                    exponents(h + 1)
                act.wait_ge(probs_ps, h + 1)
                if h >= 2:
                    act.wait_ge(attn_ps, h - 1)
                act.copy(probsT[h % 2], psum[:, 6, 0:384]).then_inc(probs_sb, 1)
                if h % 2 == 0 and h >= 2:
                    head_pair_out(h // 2 - 1)
            load_table(ACT.Sqrt)
            act.wait_ge(attn_ps, HEADS)
            act.wait_ge(pT_ps, 1)
            act.copy(pT, psum[:, 6, :].rearrange("p (c t) -> p c t", c=2)).then_inc(pT_sb, 1)
            head_pair_out(HEADS // 2 - 1)

            def ple_out(t):
                act.wait_ge(ple_ps, t + 1)
                act.copy(ple[t].rearrange("p (b n) -> p b n", b=2), psum[:, 6:8, :]).then_inc(ple_sb, 1)

            for t in range(TILES):
                for half in range(2):
                    square(1, t, half, half_of(h_sb, t, half), summed, 2 * t + half + 1)
                root_of(1, t)
            ple_out(0)
            for t in range(TILES):
                turned_out(1, t, 4 + 2 * t, hT)
            load_table(ACT.Exp)
            ple_out(1)
            act.wait_ge(exp_in, 1)
            act.activation(shifted_exp, shifted, ACT.Exp).then_inc(exp_out, 1)
            act.wait_ge(exp_in, 2)
            act.activation(tiny[:, 6, :], tiny[:, 5, :], ACT.Exp).then_inc(exp_out, 1)
            load_table(ACT.Silu)

            def moe_step(step, s):
                for q in range(QUADS_PER_STEP):
                    n = step * QUADS_PER_STEP + q
                    act.wait_ge(s["gath_ps"], n * 2 + 1)
                    act.copy(xT[:, 0:4, :], psum[:, 6, :].rearrange("p (c s) -> p c s", c=4)).then_inc(s["xT_act"], 1)
                    act.wait_ge(s["gate_ps"], n + 1)
                    act.activation(silu, psum[:, 4, :], ACT.Silu).then_inc(s["silu_ready"], 1)
                    act.wait_ge(s["hidT_ps"], n + 1)
                    act.copy(hiddenT[:, :, :], psum[:, 4, :].rearrange("p (c s) -> p c s", c=4)
                             ).then_inc(s["hidT_sb"], 1)
                    act.wait_ge(s["down_ps"], n + 1)
                    act.copy(down_sb[:, 0:512], psum[:, 6, :]).then_inc(s["down_act"], 1)

            with act.Fori(0, STEPS) as step:
                moe_step(step, main_s)
            act.wait_ge(routed, 1)
            with act.If(act.value_load(most_int[0:1, 0:1], min_val=0, max_val=SEQ) > SLOTS):
                with act.Fori(0, PASSES - 1) as again:
                    with act.Fori(0, STEPS) as step:
                        moe_step(again * STEPS + step, more_s)
                act.nop()
            load_table(ACT.Sqrt)
            for t in range(TILES):
                for half in range(2):
                    square(2, t, half, half_of(x_sb, t, half), summed, 4 + 2 * t + half + 1)
                root_of(2, t)
            load_table(ACT.Sigmoid)
            for t in range(TILES):
                turned_out(2, t, 4 + 2 * t, gateT)
            for t in range(TILES):
                for half in range(2):
                    n = 2 * t + half
                    act.wait_ge(open_ps, n + 1)
                    act.activation(half_of(h_sb, t, half), psum[:, n, :], ACT.Sigmoid).then_inc(opened, 1)
                    if half:
                        load_table(ACT.Sqrt)
                    square(3, t, half, half_of(x_sb, t, half), final_x, n + 1)
                root_of(3, t)
                if t == 0:
                    load_table(ACT.Sigmoid)

        @block.gpsimd
        def _(pool):
            pool.memset(pool_area[:, :].rearrange("p (g t) -> p g t", g=3 * POOL_GROUPS)[:, :, 0:PAD], 0.0
                        ).then_inc(padded, 1)
            pool.wait_ge(bias_row_ready, 2)
            pool.dma_start(bias_dram[:, :], bias_row).then_inc(bias_out, 16)
            pool.wait_ge(bias_out, 16)
            skewed = bass.AP(tensor=bias_dram.tensor, offset=0, ap=[[1, P], [BIAS_ROW, HEADS], [1, SEQ]])
            pool.dma_start(bias_of, skewed).then_inc(bias_in, 16)
            pool.wait_ge(normed, 2)
            pool.dma_start(gain[:, :], broadcast(a["g_ffn"][0])).then_inc(ffn_gain_in, 16)
            pool.wait_ge(turned_ps, 4)
            pool.dma_start(p_sb, p_dram).then_inc(p_in, 16)
            pool.wait_ge(route_in, 16 * (3 + GROUPS))
            pool.tensor_copy(router[:, :, 0:GROUPS], r1_sb.rearrange("p i c g -> p (i c) g")
                             ).then_inc(router_ready, 1)
            for g in range(GROUPS):
                lo = GROUPS + g * GROUP_EXPERTS
                pool.tensor_copy(router[:, :, lo:lo + GROUP_EXPERTS],
                                 r2_sb[:, g, :, :].rearrange("p i (c e) -> p (i c) e", c=2)).then_inc(router_ready, 1)
            pool.wait_ge(padded, 1)
            pool.wait_ge(z_act, 2)
            source, dest, n = u_pad, sum_a, 0
            for stage, w in enumerate(POOL_WINDOWS):
                half = w // 2
                pool.tensor_tensor(dest[:, stage:, PAD:], source[:, stage:, PAD:],
                                   source[:, stage:, PAD - half:PAD + SEQ - half], ALU.add).then_inc(pool_step, 1)
                n += 1
                pool.wait_ge(pool_step, n)
                sums = dest[:, stage, PAD:]
                pool.tensor_scalar(sums[:, PAD:], sums[:, PAD:], 1.0 / w, None, ALU.mult).then_inc(pool_step, 1)
                pool.tensor_tensor(sums[:, 0:PAD], sums[:, 0:PAD], edge[:, stage, :], ALU.mult).then_inc(pool_step, 1)
                n += 2
                pool.wait_ge(pool_step, n)
                pool.tensor_tensor(sums, sums, u_pad[:, stage, PAD:], ALU.subtract).then_inc(pooled, 1)
                source, dest = dest, (sum_b if dest is sum_a else sum_a)
            pool.wait_ge(pool_ps, POOL_GROUPS)
            pool.dma_start(g_ple, broadcast(a["g_ple"][0])).then_inc(tail_in, 16)
            pool.dma_start(g_final, broadcast(a["g_final"])).then_inc(tail_in, 16)
            pool.wait_ge(scores_ps, HEADS)
            pool.dma_start(w_ple_sb, w_ple).then_inc(w_ple_in, 16)

        @block.vector
        def _(dve):
            steps = [0]

            def done(ins):
                steps[0] += 1
                ins.then_inc(vec, 1)
                dve.wait_ge(vec, steps[0])

            done(dve.memset(eps[:, :], EPS))
            dve.memset(bias_row[:, SEQ:BIAS_ROW], MASKED).then_inc(bias_row_ready, 1)

            def base_of(which, t):
                c = 2 * which + t
                dve.wait_ge(squared, 2 * c + 1)
                dve.tensor_scalar(base[:, c:c + 1], sum_sq[:, 2 * c:2 * c + 1], 1.0 / D, EPS, ALU.mult, ALU.add
                                  ).then_inc(based, 1)

            def invert(which, t):
                c = 2 * which + t
                dve.wait_ge(rooted, c + 1)
                done(dve.reciprocal(rstd[:, c:c + 1], root[:, c:c + 1]))
                return rstd[:, c:c + 1]

            def normalise(which, t, source, gains, dest, ready):
                dve.scalar_tensor_tensor(out=dest, in0=source, scalar=invert(which, t), in1=gains,
                                         op0=ALU.mult, op1=ALU.mult).then_inc(ready, 1)

            def turned_out(which, t, bank, dest):
                dve.wait_ge(turned_ps, 4 * which + 2 * t + 2)
                dve.tensor_copy(dest[:, 4:8, t * P:(t + 1) * P],
                                psum[:, bank, :].rearrange("p (c s) -> p c s", c=4)).then_inc(turned_vec, 1)

            for t in range(TILES):
                base_of(0, t)
            dve.wait_ge(gain_in, 16)
            for t in range(TILES):
                dve.wait_ge(x_in[t], 16)
                normalise(0, t, x_sb[:, t, :], gain[:, :], h_sb[:, t, :], normed)
            for t in range(TILES):
                turned_out(0, t, 2 * t + 1, hT)
            dve.wait_ge(bias_ps, 1)
            dve.tensor_copy(bias_row[:, 0:SEQ], psum[0:HEADS, 7, 0:SEQ]).then_inc(bias_row_ready, 1)
            for b in range(2):
                dve.wait_ge(z_ps, 2 * b + 3)
                for c in range(2):
                    for t in range(TILES):
                        lo = 256 * c + 128 * t
                        last = dve.tensor_scalar(qT[:, 2 * b + c, P * t:P * t + P],
                                                 psum[:, b, lo:lo + P][:, ::-1], HEAD_DIM ** -0.5, None, ALU.mult)
                last.then_inc(z_vec, 1)

            def biased(h):
                dve.wait_ge(scores_ps, h + 1)
                if h >= 2:
                    dve.wait_ge(exped, 2 * (h - 1))
                for t in range(TILES):
                    lo, hi = (0, 128) if t == 0 else (128, 384)
                    done(dve.tensor_tensor_reduce(scores[h % 2][:, lo:hi], psum[:, 4 + h % 2, lo:hi],
                                                  bias_of[:, h, 256 - (hi - lo):256], 1.0, 3 * MASKED, ALU.add,
                                                  ALU.max, row_max[:, h, t:t + 1]))
                dve.tensor_scalar(neg_max[:, h, :], row_max[:, h, :], -1.0, None, ALU.mult).then_inc(scored, 1)

            dve.wait_ge(bias_in, 16)
            biased(0)
            biased(1)
            dve.wait_ge(z_ps, 7)
            dve.tensor_copy(v_sb[:, 0, :], psum[:, 6, :]).then_inc(z_vec, 1)
            dve.wait_ge(small_in, 32)
            for g in range(POOL_GROUPS):
                dve.wait_ge(pool_ps, 2 * (g // 2) + 2)
                dve.tensor_scalar(mixT[:, 4 + g, :], psum[:, g // 2, 256 * (g % 2):256 * (g % 2) + 256],
                                  pool_scale[:, g:g + 1], None, ALU.mult).then_inc(pool_done, 1)
            for h in range(HEADS):
                if h + 2 < HEADS:
                    biased(h + 2)
                if h % 2:
                    pair = slice(h - 1, h + 1)
                    dve.wait_ge(exped, 2 * (h + 1))
                    done(dve.reciprocal(row_inv[:, :, pair], row_sum[:, :, pair]))
                    dve.wait_ge(attn_ps, h + 1)
                    dve.tensor_tensor(
                        h_sb[:, :, (h - 1) * HEAD_DIM:(h + 1) * HEAD_DIM].rearrange("p t (h d) -> p t h d", h=2),
                        psum[:, 7, 0:256].rearrange("p (t h d) -> p t h d", t=TILES, h=2),
                        row_inv[:, :, pair].unsqueeze(3).broadcast_to([P, TILES, 2, HEAD_DIM]),
                        ALU.mult).then_inc(attn_sb, 1)
            dve.wait_ge(attnT_ps, HEADS // 2)
            dve.wait_ge(pT_ps, 1)
            for t in range(TILES):
                for half in range(2):
                    dve.wait_ge(mix_ps, 2 * t + half + 1)
                    dve.tensor_tensor(half_of(h_sb, t, half), half_of(x_sb, t, half), psum[:, 2 * t + half, :],
                                      ALU.add).then_inc(summed, 1)
                base_of(1, t)
            dve.wait_ge(ffn_gain_in, 16)
            dve.wait_ge(summed, 4)
            for t in range(TILES):
                normalise(1, t, h_sb[:, t, :], gain[:, :], h_sb[:, t, :], normed)
            for t in range(TILES):
                turned_out(1, t, 5 + 2 * t, hT)

            def row(i):
                return small[:, i, :, :]

            def spread(v, n):
                return v.unsqueeze(2).broadcast_to([P, TILES, n])

            dve.wait_ge(route_in, 16 * (3 + GROUPS))
            dve.wait_ge(logitsT_ps, 1)
            dve.tensor_scalar(logitsT, psum[0:GROUPS + EXPERTS, 4, 0:SEQ], router_bias[:, 0:1], None, ALU.add
                              ).then_inc(logitsT_sb, 1)
            dve.wait_ge(logits_ps, 1)
            done(dve.tensor_copy(logits[:, :, 0:GROUPS + EXPERTS],
                                 psum[:, 5, 0:128].rearrange("p (t n) -> p t n", t=TILES)[:, :, 0:GROUPS + EXPERTS]))
            group_logits, expert_logits = logits[:, :, 0:GROUPS], logits[:, :, GROUPS:GROUPS + EXPERTS]

            def one_hot(values, n, top, dest, scratch):
                done(dve.tensor_reduce(top, values, AX, ALU.max))
                done(dve.tensor_tensor(dest, values, spread(top, n), ALU.is_equal))
                done(dve.tensor_tensor(dest, dest, first[:, 0:n].unsqueeze(1).broadcast_to([P, TILES, n]), ALU.mult))
                done(dve.tensor_reduce(scratch, dest, AX, ALU.max))
                done(dve.tensor_tensor(dest, dest, spread(scratch, n), ALU.is_equal))

            top_g, top_1, top_2, scratch_top = (tiny[:, i, :] for i in range(4))
            one_hot(group_logits, GROUPS, top_g, in_group, scratch_top)
            dve.tensor_tensor(shifted, group_logits, spread(top_g, GROUPS), ALU.subtract).then_inc(exp_in, 1)
            done(dve.tensor_scalar(penalty, in_group, -1.0, -MASKED, ALU.add, ALU.mult))
            kept = row(3)
            done(dve.tensor_tensor(kept.rearrange("p t (g e) -> p t g e", g=GROUPS),
                                   expert_logits.rearrange("p t (g e) -> p t g e", g=GROUPS),
                                   penalty.unsqueeze(3).broadcast_to([P, TILES, GROUPS, GROUP_EXPERTS]),
                                   ALU.add))
            best, second = row(4), row(5)
            one_hot(kept, EXPERTS, top_1, best, scratch_top)
            done(dve.scalar_tensor_tensor(out=kept, in0=best, scalar=MASKED, in1=kept, op0=ALU.mult, op1=ALU.add))
            one_hot(kept, EXPERTS, top_2, second, scratch_top)
            taken, no_slot = row(6), row(9)
            dve.tensor_tensor(taken, best, second, ALU.add).then_inc(chosen, 1)
            dve.tensor_tensor(tiny[:, 5, :], top_2, top_1, ALU.subtract).then_inc(exp_in, 1)
            dve.wait_ge(chosen, 1)
            done(dve.tensor_scalar(no_slot, taken, -NO_SLOT, NO_SLOT, ALU.mult, ALU.add))
            dve.wait_ge(exp_out, 1)
            done(dve.tensor_reduce(tiny[:, 7, :], shifted_exp, AX, ALU.add))
            done(dve.reciprocal(tiny[:, 8, :], tiny[:, 7, :]))
            dve.wait_ge(exp_out, 2)
            done(dve.tensor_scalar(tiny[:, 9, :], tiny[:, 6, :], 1.0, None, ALU.add))
            done(dve.reciprocal(tiny[:, 10, :], tiny[:, 9, :]))
            done(dve.tensor_tensor(tiny[:, 11, :], tiny[:, 10, :], tiny[:, 8, :], ALU.mult))
            done(dve.tensor_tensor(tiny[:, 12, :], tiny[:, 11, :], tiny[:, 6, :], ALU.mult))
            gates = row(7)
            done(dve.tensor_tensor(gates, best, spread(tiny[:, 11, :], EXPERTS), ALU.mult))
            done(dve.tensor_tensor(row(8), second, spread(tiny[:, 12, :], EXPERTS), ALU.mult))
            done(dve.tensor_tensor(gates, gates, row(8), ALU.add))
            dve.wait_ge(rank_ps, 1)
            done(dve.tensor_tensor(ranks[:, :, :], psum[:, 5, 0:64].rearrange("p (t e) -> p t e", t=TILES),
                                   no_slot, ALU.add))
            done(dve.tensor_reduce(most[:, :], psum[:, 5, 64:96], AX, ALU.max))
            dve.tensor_copy(most_int[:, :], most[:, :]).then_inc(routed, 1)

            def moe_step(step, quad0, s, moved_on=None):
                if moved_on is not None:
                    dve.wait_ge(next_ranks, moved_on)
                for q in range(QUADS_PER_STEP):
                    n = step * QUADS_PER_STEP + q
                    e0 = (quad0 + q) * QUAD

                    def of_quad(v):
                        return v[:, :, bass.ds(e0, QUAD)].unsqueeze(3).broadcast_to([P, TILES, QUAD, SLOTS])

                    dve.tensor_tensor(select, of_quad(ranks[:, :, :]),
                                      slot_no.unsqueeze(1).unsqueeze(1).broadcast_to([P, TILES, QUAD, SLOTS]),
                                      ALU.is_equal).then_inc(s["selected"], 1)
                    dve.wait_ge(s["selected"], n + 1)
                    dve.tensor_tensor(weighted, select, of_quad(gates), ALU.mult).then_inc(s["sel_ready"], 1)
                    dve.wait_ge(s["gath_ps"], n * 2 + 2)
                    dve.tensor_copy(xT[:, 4:8, :], psum[:, 7, :].rearrange("p (c s) -> p c s", c=4)
                                    ).then_inc(s["xT_vec"], 1)
                    dve.wait_ge(s["scat_ps"], n + 1)
                    dve.tensor_copy(scatterT, psum[:, 5, 0:256]).then_inc(s["scat_sb"], 1)
                    dve.wait_ge(s["silu_ready"], n + 1)
                    dve.wait_ge(s["up_ps"], n + 1)
                    dve.tensor_tensor(hidden, silu, psum[:, 5, :], ALU.mult).then_inc(s["hid_ready"], 1)
                    dve.wait_ge(s["down_ps"], n + 1)
                    dve.tensor_copy(down_sb[:, 512:1024], psum[:, 7, :]).then_inc(s["down_vec"], 1)

            dve.wait_ge(routed, 1)
            with dve.Fori(0, STEPS) as step:
                moe_step(step, step * QUADS_PER_STEP, main_s)
            with dve.If(dve.value_load(most_int[0:1, 0:1], min_val=0, max_val=SEQ) > SLOTS):
                with dve.Fori(0, PASSES - 1) as again:
                    dve.tensor_scalar(ranks[:, :, :], ranks[:, :, :], float(-SLOTS), None, ALU.add
                                      ).then_inc(next_ranks, 1)
                    with dve.Fori(0, STEPS) as step:
                        moe_step(again * STEPS + step, step * QUADS_PER_STEP, more_s, again + 1)
                dve.wait_ge(more_s["scattered"], (PASSES - 1) * 2 * EXPERTS // QUAD)
                dve.nop()

            for t in range(TILES):
                dve.wait_ge(main_s["scattered"], 2 * EXPERTS // QUAD - 1 + t)
                for half in range(2):
                    dve.tensor_tensor(half_of(x_sb, t, half), half_of(x_sb, t, half), psum[:, 2 * t + half, :],
                                      ALU.add).then_inc(summed, 1)
                base_of(2, t)
            dve.wait_ge(summed, 8)
            dve.wait_ge(tail_in, 32)
            for t in range(TILES):
                normalise(2, t, x_sb[:, t, :], g_ple, h_sb[:, t, :], normed)
            for t in range(TILES):
                turned_out(2, t, 5 + 2 * t, gateT)
            dve.wait_ge(ple_sb, 2)
            for t in range(TILES):
                for half in range(2):
                    n = 2 * t + half
                    gate, x_half = half_of(h_sb, t, half), half_of(x_sb, t, half)
                    dve.wait_ge(opened, n + 1)
                    done(dve.tensor_tensor(gate, gate, ple[t][:, 512 * half:512 * half + 512], ALU.mult))
                    dve.tensor_tensor(x_half, x_half, gate, ALU.add).then_inc(final_x, 1)
                    if half == 0:
                        base_of(3, t)
                scale = invert(3, t)
                for half in range(2):
                    dve.scalar_tensor_tensor(out=half_of(h_sb, t, half), in0=half_of(x_sb, t, half), scalar=scale,
                                             in1=g_final[:, 512 * half:512 * half + 512], op0=ALU.mult,
                                             op1=ALU.mult).then_inc(final_out, 1)

        @block.tensor
        def _(pe):
            def turn(which, t, banks, columns):
                pe.wait_ge(normed, 2 * which + t + 1)
                if which == 1 and t == 1:
                    pe.wait_ge(ple_sb, 1)
                for c in range(8):
                    last = pe.transpose(psum[:, banks[c // 4], P * (c % 4):P * (c % 4) + P], columns(t, c), ident)
                    if which == 1 and t == 0 and c <= W_OUT_UNITS:
                        last.then_inc(ring_free, 1)
                    if c % 4 == 3:
                        last.then_inc(turned_ps, 1)

            def pairs(t, c):
                i, c2 = divmod(c, 2)
                return h_sb[:, t, 256 * i + c2:256 * i + 256:2]

            def plain(t, c):
                return h_sb[:, t, P * c:P * c + P]

            pe.wait_ge(consts_in, 16)
            for t in range(TILES):
                turn(0, t, (2 * t, 2 * t + 1), pairs)
            pe.wait_ge(early_in, 32)
            pe.matmul(psum[0:HEADS, 7, 0:SEQ], rel_bias[:, :], bucket_of, start=True, stop=True).then_inc(bias_ps, 1)

            chunk_bank = {**{c: c // 2 for c in range(8)}, **{12 + g: 4 + g // 2 for g in range(4)}}
            order = [12, 13, 14, 15, 0, 1, 4, 5, 2, 3, 6, 7]
            w = [unit(i).rearrange("p (c n) -> p c n", c=2) for i in range(W_IN_UNITS)]

            def project(c, m):
                half = SEQ * (m % 2)
                return pe.matmul(psum[:, chunk_bank[m], half:half + SEQ], w[c // 2][:, c % 2, P * m:P * m + P],
                                 hT[:, c, :], start=(c == 0 and m % 2 == 0), stop=(c == 7), skip_group_check=True)

            def project_v(c, t):
                return pe.matmul(psum[:, 6 + t, :], hT[:, c, t * P:(t + 1) * P], w[c // 2][:, c % 2, 1024:1536],
                                 start=(c == 0), stop=(c == 7), skip_group_check=True)

            pe.wait_ge(turned_act, 2)
            pe.wait_ge(turned_vec, 2)
            for c in range(6):
                if c % 2 == 0:
                    pe.wait_ge(slot_in[c // 2], 16)
                for m in order:
                    project(c, m)
            pe.wait_ge(slot_in[3], 16)
            for i in range(0, 12, 2):
                for m in order[i:i + 2]:
                    for c in (6, 7):
                        last = project(c, m)
                last.then_inc(z_ps, 1)

            def score(h):
                r = HEAD_DIM * (h % 2)
                q_h, k_h = (v[r:r + HEAD_DIM, h // 2, :] for v in (qT, kT))
                if h >= 2:
                    pe.wait_ge(scored, h - 1)
                pe.matmul(psum[:, 4 + h % 2, 0:128], q_h[:, 0:P], k_h[:, 0:P], start=True, stop=True)
                pe.matmul(psum[:, 4 + h % 2, 128:384], q_h[:, P:], k_h, start=True, stop=True).then_inc(scores_ps, 1)

            def mix(c, t, first_one, last_one):
                w_c = unit(W_IN_UNITS + c // 4).rearrange("p (c n) -> p c n", c=4)[:, c % 4, :]
                for half in range(2):
                    last = pe.matmul(psum[:, 2 * t + half, :], mixT[:, c, t * P:(t + 1) * P],
                                     w_c[:, 512 * half:512 * half + 512], start=first_one, stop=last_one,
                                     skip_group_check=True)
                    if last_one:
                        last.then_inc(mix_ps, 1)

            def turn_probs(h):
                pe.wait_ge(exped, 2 * (h + 1))
                if h >= 1:
                    pe.wait_ge(probs_sb, h)
                for i in range(3):
                    last = pe.transpose(psum[:, 6, P * i:P * i + P], probs[h % 2][:, P * i:P * i + P], ident)
                last.then_inc(probs_ps, 1)

            def turn_pair(pair):
                pe.wait_ge(attn_sb, pair + 1)
                for t in range(TILES):
                    last = pe.transpose(psum[:, 7, 256 + P * t:256 + P * t + P],
                                        h_sb[:, t, pair * P:(pair + 1) * P], flip)
                last.then_inc(attnT_ps, 1)

            def attend(h):
                pe.wait_ge(probs_sb, h + 1)
                if h % 2 == 0 and h >= 2:
                    pe.wait_ge(attnT_sb, h // 2)
                o = psum[:, 7, 0:256].rearrange("p (t h d) -> p t h d", t=TILES, h=2)
                values = v_sb[:, :, h * HEAD_DIM:(h + 1) * HEAD_DIM]
                pe.matmul(o[:, 0, h % 2, :], probsT[h % 2][:, 0:P], values[:, 0, :], start=True, stop=True)
                pe.matmul(o[:, 1, h % 2, :], probsT[h % 2][:, P:2 * P], values[:, 0, :], start=True, stop=False)
                pe.matmul(o[:, 1, h % 2, :], probsT[h % 2][:, 2 * P:], values[:, 1, :], start=False, stop=True
                          ).then_inc(attn_ps, 1)

            pe.wait_ge(z_vec, 2)
            pe.wait_ge(z_act, 4)
            score(0)
            score(1)
            for c in range(8):
                for t in range(TILES):
                    last = project_v(c, t)
                    if t == 0 and c % 2 == 0 and c > 0:
                        last.then_inc(ring_free, 1)
                    if c == 7:
                        last.then_inc(z_ps, 1)
            pe.wait_ge(small_in, 32)
            for g in range(POOL_GROUPS):
                pe.wait_ge(pooled, g + 1)
                pe.matmul(psum[:, g // 2, 256 * (g % 2):256 * (g % 2) + 256], w_pool[:, g, :],
                          (sum_a, sum_b)[g % 2][:, g, PAD:], start=True, stop=True).then_inc(pool_ps, 1)
            pe.wait_ge(slot_in[4], 16)
            pe.wait_ge(slot_in[5], 16)
            pe.wait_ge(z_vec, 3)
            for h in range(HEADS):
                turn_probs(h)
                if h % 2 == 0 and h >= 2:
                    turn_pair(h // 2 - 1)
                if h + 2 < HEADS:
                    score(h + 2)
                if h == 0:
                    pe.wait_ge(z_act, 5)
                    pe.wait_ge(pool_done, POOL_GROUPS)
                if h < 4:
                    for t in range(TILES):
                        mix(4 + h, t, h == 0, False)
                elif h in (4, 5):
                    pe.wait_ge(attnT_sb, h - 3)
                    for t in range(TILES):
                        mix(h - 4, t, False, False)
                elif h == 7:
                    mix(2, 0, False, False)
                attend(h)
            mix(2, 1, False, False)
            pe.wait_ge(p_in, 16)
            pe.wait_ge(probs_sb, HEADS)
            for c in range(2):
                for t in range(TILES):
                    last = pe.transpose(psum[:, 6, SEQ * c + P * t:SEQ * c + P * t + P],
                                        p_sb[:, t, c * P:(c + 1) * P], ident)
            last.then_inc(pT_ps, 1)
            turn_pair(3)
            pe.wait_ge(attnT_sb, 4)
            for t in range(TILES):
                mix(3, t, False, True)

            def embed(t):
                if t:
                    pe.wait_ge(ple_sb, t)
                for half in range(2):
                    for c in range(2):
                        last = pe.matmul(psum[:, 6 + half, :], pT[:, c, t * P:(t + 1) * P],
                                         w_ple_sb[:, c, 512 * half:512 * half + 512], start=(c == 0), stop=(c == 1))
                last.then_inc(ple_ps, 1)

            pe.wait_ge(pT_sb, 1)
            pe.wait_ge(w_ple_in, 16)
            embed(0)

            for t in range(TILES):
                turn(1, t, (4 + 2 * t, 5 + 2 * t), pairs)
            pe.wait_ge(router_ready, 1 + GROUPS)
            pe.wait_ge(turned_act, 4)
            pe.wait_ge(turned_vec, 4)
            for c in range(8):
                last = pe.matmul(psum[0:GROUPS + EXPERTS, 4, 0:SEQ], router[:, c, :], hT[:, c, :],
                                 start=(c == 0), stop=(c == 7))
            last.then_inc(logitsT_ps, 1)
            pe.wait_ge(logitsT_sb, 1)
            for t in range(TILES):
                last = pe.transpose(psum[:, 5, 64 * t:64 * t + GROUPS + EXPERTS], logitsT[:, t * P:(t + 1) * P],
                                    ident[0:GROUPS + EXPERTS, 0:GROUPS + EXPERTS])
            last.then_inc(logits_ps, 1)
            embed(1)
            pe.wait_ge(chosen, 1)
            taken = small[:, 6, :, :]
            pe.matmul(psum[:, 5, 0:32], earlier, taken[:, 0, :], start=True, stop=True)
            pe.matmul(psum[:, 5, 32:64], earlier, taken[:, 1, :], start=True, stop=False)
            pe.matmul(psum[:, 5, 32:64], ones, taken[:, 0, :], start=False, stop=True)
            pe.matmul(psum[:, 5, 64:96], ones, taken[:, 0, :], start=True, stop=False)
            pe.matmul(psum[:, 5, 64:96], ones, taken[:, 1, :], start=False, stop=True).then_inc(rank_ps, 1)

            def moe_step(step, s, arrived, free, earlier_uses):
                def unit_in(u):
                    slot = (FIRST_EXPERT_UNIT + u) % RING
                    pe.wait_ge(arrived[slot], step * (16 * STEP_USES) + 16 * (earlier_uses[slot] + u // RING + 1))
                    return expert_unit(slot)

                def strips(bank, lhsT, w_u, lo, start, stop, used_before):
                    for e in range(QUAD):
                        last = pe.matmul(psum[SLOTS * e:SLOTS * e + SLOTS, bank, :],
                                         lhsT[:, SLOTS * e:SLOTS * e + SLOTS], w_u[:, e, lo:lo + 512],
                                         start=start, stop=stop, skip_group_check=True)
                        if used_before and e == 0:
                            last.then_inc(free, 1)
                    return last

                for q in range(QUADS_PER_STEP):
                    n = step * QUADS_PER_STEP + q
                    pe.wait_ge(s["selected"], n + 1)
                    for c in range(8):
                        for t in range(TILES):
                            last = pe.matmul(psum[:, 6 + c // 4, P * (c % 4):P * (c % 4) + P], pairs(t, c),
                                             select[:, t, :, :], start=(t == 0), stop=(t == 1))
                        if c % 4 == 3:
                            last.then_inc(s["gath_ps"], 1)
                    pe.wait_ge(s["xT_act"], n + 1)
                    for kind, name in enumerate(("gate_ps", "up_ps")):
                        for i in range(4):
                            if (kind, i) == (0, 2):
                                pe.wait_ge(s["sel_ready"], n + 1)
                                for t in range(TILES):
                                    last = pe.matmul(psum[:, 5, P * t:P * t + P], weighted[:, t, :, :], ident,
                                                     start=True, stop=True)
                                last.then_inc(s["scat_ps"], 1)
                                pe.wait_ge(s["xT_vec"], n + 1)
                            if (kind, i) == (1, 0):
                                pe.wait_ge(s["scat_sb"], n + 1)
                            w_u = unit_in(q * QUAD_UNITS + 4 * kind + i)
                            for c2 in range(2):
                                last = strips(4 + kind, xT[:, 2 * i + c2, :], w_u, 512 * c2, i + c2 == 0,
                                              i == 3 and c2 == 1, c2 == 0 and (kind, i) != (0, 0))
                        last.then_inc(s[name], 1)
                    pe.wait_ge(s["hid_ready"], n + 1)
                    for c in range(4):
                        last = pe.transpose(psum[:, 4, P * c:P * c + P], hidden[:, P * c:P * c + P], ident)
                        if c == 0:
                            last.then_inc(free, 1)
                    last.then_inc(s["hidT_ps"], 1)
                    pe.wait_ge(s["hidT_sb"], n + 1)
                    for i in range(4):
                        w_u = unit_in(q * QUAD_UNITS + 8 + i)
                        for half in range(2):
                            last = strips(6 + half, hiddenT[:, i, :], w_u, 512 * half, i == 0, i == 3,
                                          half == 0 and i > 0)
                    last.then_inc(s["down_ps"], 1)
                    pe.wait_ge(s["down_act"], n + 1)
                    pe.wait_ge(s["down_vec"], n + 1)
                    for t in range(TILES):
                        for half in range(2):
                            last = pe.matmul(psum[:, 2 * t + half, :], scatterT[:, t * P:(t + 1) * P],
                                             down_sb[:, 512 * half:512 * half + 512], start=False, stop=False,
                                             skip_group_check=True)
                            if t + half == 0:
                                last.then_inc(free, 1)
                        last.then_inc(s["scattered"], 1)

            with pe.Fori(0, STEPS) as step:
                moe_step(step, main_s, slot_in, ring_free, [int(i < FIRST_EXPERT_UNIT) for i in range(RING)])
            pe.wait_ge(routed, 1)
            with pe.If(pe.value_load(most_int[0:1, 0:1], min_val=0, max_val=SEQ) > SLOTS):
                with pe.Fori(0, PASSES - 1) as again:
                    with pe.Fori(0, STEPS) as step:
                        moe_step(again * STEPS + step, more_s, more_in, more_free, [0] * RING)
                pe.nop()

            for t in range(TILES):
                turn(2, t, (4 + 2 * t, 5 + 2 * t), plain)
            w_g = []
            for n in range(FIRST_EXPERT_UNIT + EXPERT_UNITS, FIRST_EXPERT_UNIT + EXPERT_UNITS + 2):
                pe.wait_ge(slot_in[n % RING], 16 * (n // RING + 1))
                w_g.append(unit(n % RING).rearrange("p (c n) -> p c n", c=4))
            for t in range(TILES):
                pe.wait_ge(turned_act, 5 + t)
                pe.wait_ge(turned_vec, 5 + t)
                for half in range(2):
                    for c in range(8):
                        last = pe.matmul(psum[:, 2 * t + half, :], gateT[:, c, t * P:(t + 1) * P],
                                         w_g[c // 4][:, c % 4, 512 * half:512 * half + 512],
                                         start=(c == 0), stop=(c == 7))
                    last.then_inc(open_ps, 1)


def constant_table():
    import math
    table = np.zeros((P, C_KEPT + SEQ), np.float32)
    table[:, C_IDENT:C_IDENT + P] = np.eye(P)
    table[:, C_EARLIER:C_EARLIER + P] = np.triu(np.ones((P, P)), 1)
    table[:, C_ONES:C_ONES + P] = 1.0
    table[:, C_SLOT:C_SLOT + SLOTS] = np.arange(SLOTS)
    table[:, C_FIRST:C_FIRST + EXPERTS] = EXPERTS - np.arange(EXPERTS)
    for g, w in enumerate(POOL_WINDOWS):
        table[:, C_EDGE + PAD * g:C_EDGE + PAD * (g + 1)] = 1.0 / np.minimum(np.arange(PAD) + 1, w)
    table[:, C_FLIP:C_FLIP + P] = np.eye(P)[::-1]
    distance = SEQ - 1 - np.arange(SEQ)
    exact = BUCKETS // 2
    far = np.log(np.maximum(distance, 1).astype(np.float32) / np.float32(exact))
    far = far / np.float32(math.log(MAX_DIST / exact)) * np.float32(BUCKETS - exact)
    bucket = np.where(distance < exact, distance, np.minimum(exact + far.astype(np.int32), BUCKETS - 1))
    table[bucket, C_KEPT + np.arange(SEQ)] = 1.0
    return table


INPUTS = ["x", "p", "g_mix", "w_in", "w_pool", "pool_scale", "w_out", "rel_bias", "g_ffn", "w_r1", "b_r1", "w_r2",
          "b_r2", "w_gate", "w_up", "w_down", "g_ple", "w_ple_proj", "w_ple_gate", "g_final"]


def kernel(**inputs):
    import concourse.bacc as bacc
    from concourse.bass_utils import run_bass_kernel_spmd

    nc = bacc.Bacc("TRN2", target_bir_lowering=False, num_devices=1)
    arrays, aps = {}, {}
    for name in [*INPUTS, "consts"]:
        array = constant_table() if name == "consts" else np.ascontiguousarray(inputs[name])
        arrays[f"in_{name}"] = array
        aps[name] = nc.dram_tensor(f"in_{name}", array.shape, mybir.dt.from_np(array.dtype), kind="ExternalInput").ap()
    out = nc.dram_tensor("out_x", (1, SEQ, D), F32, kind="ExternalOutput").ap()
    layer_kernel(nc, aps, out)
    result = run_bass_kernel_spmd(nc, [arrays], core_ids=[0])
    return result.results[0]["out_x"]
```

```python
from contextlib import ExitStack

import numpy as np

import concourse.bass as bass
from concourse import mybir

F32 = mybir.dt.float32
I32 = mybir.dt.int32
ALU = mybir.AluOpType
ACT = mybir.ActivationFunctionType
AX = mybir.AxisListType.X

P = 128
SEQ = 256
TILES = SEQ // P
D = 1024
HEADS, HEAD_DIM = 8, 64
D_ATTN = HEADS * HEAD_DIM
GROUPS, GROUP_EXPERTS, D_EXPERT = 4, 8, 512
EXPERTS = GROUPS * GROUP_EXPERTS
QUAD = 4
SLOTS = 32
QUADS_PER_STEP = 2
STEPS = EXPERTS // QUAD // QUADS_PER_STEP
PASSES = SEQ // SLOTS
D_PLE = 256
POOL_WINDOWS = (2, 4, 8, 16)
POOL_GROUPS = len(POOL_WINDOWS)
PAD = 16
BUCKETS, MAX_DIST = 32, 128
EPS = 1e-6
MASKED = -1e30
RING = 8
UNIT = 4096
W_IN_UNITS, W_OUT_UNITS, QUAD_UNITS = 4, 2, 12
EARLY = (4, 2, 6)
FIRST_EXPERT_UNIT = W_IN_UNITS + W_OUT_UNITS - len(EARLY)
STEP_UNITS = QUADS_PER_STEP * QUAD_UNITS
STEP_USES = STEP_UNITS // RING
EXPERT_UNITS = STEPS * STEP_UNITS
BIAS_ROW = 384
NO_SLOT = 1000.0
MIX_BETWEEN = (((4, 0), (4, 1)), ((5, 0), (5, 1)), ((6, 0),), ((6, 1),), ((7, 0),), ((7, 1),),
               ((0, 0), (0, 1)), ((1, 0), (1, 1)))
PIECES = ((0, 0, 512, 0), (0, 512, 1024, 1), (1, 0, 512, 2), (1, 512, 768, 3), (1, 768, 1024, 0))
PLE_BANKS = ((5, 4), (6, 5))

C_IDENT, C_FLIP, C_EARLIER, C_ONES, C_SLOT, C_FIRST, C_EDGE = 0, 128, 256, 384, 512, 544, 576
C_KEPT = C_EDGE + POOL_GROUPS * PAD


def layer_kernel(nc, a, out):
    with ExitStack() as ctx:
        def sbuf(name, cols, dt=F32, rows=P):
            return ctx.enter_context(nc.sbuf_tensor(name, [rows, cols], dt))

        def sem(name):
            return ctx.enter_context(nc.semaphore(name))

        ring = ctx.enter_context(nc.sbuf_tensor("ring", [P, RING, UNIT], F32))
        x_sb = ctx.enter_context(nc.sbuf_tensor("x_sb", [P, TILES, D], F32))
        h_sb = ctx.enter_context(nc.sbuf_tensor("h_sb", [P, TILES, D], F32))
        hT = ctx.enter_context(nc.sbuf_tensor("hT", [P, 8, SEQ], F32))
        qk_area = sbuf("qk_area", 2048)
        v_area = sbuf("v_area", 1024)
        bias_area = sbuf("bias_area", 2048)
        pool_area = sbuf("pool_area", 2816 + 512)
        attn_area = sbuf("attn_area", 2304)
        gains = ctx.enter_context(nc.sbuf_tensor("gains", [P, 3, 8], F32))
        g_final = sbuf("g_final_sb", D)
        consts = sbuf("consts", C_KEPT)
        w_pool = ctx.enter_context(nc.sbuf_tensor("w_pool_sb", [P, POOL_GROUPS, P], F32))
        pool_scale = sbuf("pool_scale_sb", POOL_GROUPS)
        router = ctx.enter_context(nc.sbuf_tensor("router", [P, 8, GROUPS + EXPERTS], F32))
        router_bias = sbuf("router_bias", GROUPS + EXPERTS)
        rel_bias = sbuf("rel_bias_sb", HEADS, rows=BUCKETS)
        eps = sbuf("eps", 1)
        warm = sbuf("warm", 16)
        sum_sq = sbuf("sum_sq", 16)
        base = sbuf("base", 8)
        root = sbuf("root", 8)
        rstd = sbuf("rstd", 8)
        row_max = ctx.enter_context(nc.sbuf_tensor("row_max", [P, HEADS, TILES], F32))
        neg_max = ctx.enter_context(nc.sbuf_tensor("neg_max", [P, HEADS, TILES], F32))
        row_sum = ctx.enter_context(nc.sbuf_tensor("row_sum", [P, TILES, HEADS], F32))
        row_inv = ctx.enter_context(nc.sbuf_tensor("row_inv", [P, TILES, HEADS], F32))
        routing = sbuf("routing", 12 * TILES * EXPERTS)
        tiny = ctx.enter_context(nc.sbuf_tensor("tiny", [P, 16, TILES], F32))
        ranks = ctx.enter_context(nc.sbuf_tensor("ranks", [P, TILES, EXPERTS], F32))
        most = tiny[:, 15, 0:1]
        most_int = sbuf("most_int", 1, I32)

        ident = consts[:, C_IDENT:C_IDENT + P]
        flip = consts[:, C_FLIP:C_FLIP + P]
        earlier = consts[:, C_EARLIER:C_EARLIER + P]
        ones = consts[:, C_ONES:C_ONES + P]
        slot_no = consts[:, C_SLOT:C_SLOT + SLOTS]
        first = consts[:, C_FIRST:C_FIRST + EXPERTS]
        edge = consts[:, C_EDGE:C_KEPT].rearrange("p (g t) -> p g t", g=POOL_GROUPS)

        small = routing[:, :].rearrange("p (i t e) -> p i t e", i=12, t=TILES)
        r1_sb = routing[:, 0:32].rearrange("p (i c g) -> p i c g", i=4, c=2)
        r2_sb = routing[:, 32:288].rearrange("p (g i c) -> p g i c", g=GROUPS, i=4)
        logits = routing[:, 0:128].rearrange("p (t n) -> p t n", t=TILES)
        shifted, shifted_exp, other_group = (
            routing[:, 128 + 8 * i:136 + 8 * i].rearrange("p (t n) -> p t n", t=TILES) for i in range(3))
        logitsT = routing[0:GROUPS + EXPERTS, 512:768]

        qT = qk_area[:, 0:1024].rearrange("p (c t) -> p c t", c=4)
        kT = qk_area[:, 1024:2048].rearrange("p (c t) -> p c t", c=4)
        down_sb = qk_area[:, 0:1024]
        filler = hT[:, 0, 0:P]
        bucket_of = v_area[0:BUCKETS, 0:SEQ]
        bias_row = v_area[0:HEADS, SEQ:SEQ + BIAS_ROW]
        v_sb = v_area[:, :].rearrange("p (t n) -> p t n", t=TILES)
        ple = [v_area[:, :], hT[:, 0:4, :].rearrange("p c t -> p (c t)")]
        bias_of = bias_area[:, :].rearrange("p (h k) -> p h k", h=HEADS)
        xT = bias_area[:, 0:1024].rearrange("p (c s) -> p c s", c=8)
        hidden = bias_area[:, 1024:1536]
        hiddenT = bias_area[:, 1536:2048].rearrange("p (c s) -> p c s", c=4)
        width = POOL_GROUPS * (SEQ + PAD)
        u_pad, sum_a, sum_b = (pool_area[:, i * width:(i + 1) * width].rearrange("p (g t) -> p g t", g=POOL_GROUPS)
                               for i in range(3))
        select = pool_area[:, 0:256].rearrange("p (t e s) -> p t e s", t=TILES, e=QUAD)
        weighted = pool_area[:, 256:512].rearrange("p (t e s) -> p t e s", t=TILES, e=QUAD)
        scatterT = pool_area[:, 512:768]
        w_ple_sb = bias_area[:, :].rearrange("p (c n) -> p c n", c=2)
        early_place = [
            [[pool_area[:, 768:1792]], [pool_area[:, 1792:2816]], [qk_area[:, 0:1024]], [qk_area[:, 1024:2048]]],
            [[attn_area[:, 0:1024]], [attn_area[:, 1024:2048]], [hT[:, 4:8, :].rearrange("p c t -> p (c t)")],
             [bias_area[:, 1024:2048]]],
            [[x_sb[:, 0, :]], [x_sb[:, 1, :]], [g_final[:, :]],
             [w_pool[:, :, :].rearrange("p g n -> p (g n)"), pool_area[:, 2816:3328]]]]
        scores = [attn_area[:, 384 * i:384 * i + 384] for i in range(2)]
        probs = [attn_area[:, 768 + 384 * i:768 + 384 * i + 384] for i in range(2)]
        probsT = [attn_area[:, 1536 + 384 * i:1536 + 384 * i + 384] for i in range(2)]
        silu = attn_area[:, 0:512]
        scratch = attn_area[:, 0:1024]
        g_final_row = attn_area[0:1, 1024:2048]
        pT = attn_area[:, 1536:2048].rearrange("p (c t) -> p c t", c=2)
        p_sb = h_sb[:, 0, 512:1024].rearrange("p (t n) -> p t n", t=TILES)
        gateT = bias_area[:, :].rearrange("p (c t) -> p c t", c=8)
        mixT = hT

        psum = ctx.enter_context(nc.psum_tensor("psum", [P, 8, 512], F32))

        bias_dram = nc.dram_tensor("bias_by_distance", [HEADS, BIAS_ROW], F32, kind="Internal").ap()

        x_in = [sem(f"x_in{t}") for t in range(TILES)]
        ident_in, consts_in, bucket_in, gains_in, later_gains_in = map(
            sem, ("ident_in", "consts_in", "bucket_in", "gains_in", "later_gains_in"))
        small_in, route_in = sem("small_in"), sem("route_in")
        bias_out, bias_in, gain_row_in, p_in, w_ple_in, out_done = map(
            sem, ("bias_out", "bias_in", "gain_row_in", "p_in", "w_ple_in", "out_done"))
        slot_in = [sem(f"slot_in{s}") for s in range(RING)]
        more_in = [sem(f"more_in{s}") for s in range(RING)]
        ring_free, more_free = sem("ring_free"), sem("more_free")
        vec = sem("vector_step")
        squared, squared_vec, based, rooted, inverted, normed = map(
            sem, ("squared", "squared_vec", "based", "rooted", "inverted", "normed"))
        scaled = [sem(f"scaled{t}") for t in range(TILES)]
        turned_ps, turned_act, turned_vec = map(sem, ("turned_ps", "turned_act", "turned_vec"))
        summed, filler_ready = sem("summed"), sem("filler_ready")
        bias_ps, bias_row_ready = map(sem, ("bias_ps", "bias_row_ready"))
        z_ps, z_act, z_vec = map(sem, ("z_ps", "z_act", "z_vec"))
        pooled, pool_step, pool_ps, pool_done, padded = map(
            sem, ("pooled", "pool_step", "pool_ps", "pool_done", "padded"))
        router_ready = sem("router_ready")
        scores_ps, scored, exped, probs_ps, probs_sb = map(
            sem, ("scores_ps", "scored", "exped", "probs_ps", "probs_sb"))
        attn_ps, attn_sb, attnT_ps, attnT_sb, mix_ps = map(
            sem, ("attn_ps", "attn_sb", "attnT_ps", "attnT_sb", "mix_ps"))
        logitsT_ps, logitsT_sb, logits_ps, exp_in, exp_out, chosen, rank_ps, routed = map(
            sem, ("logitsT_ps", "logitsT_sb", "logits_ps", "exp_in", "exp_out", "chosen", "rank_ps", "routed"))
        pT_ps, pT_sb, ple_ps, ple_sb = map(sem, ("pT_ps", "pT_sb", "ple_ps", "ple_sb"))
        open_ps, opened, final_x, gained, final_out, final_out_act = map(
            sem, ("gate_logits_ps", "gate_opened", "final_x", "gained", "final_out", "final_out_act"))

        names = ("selected", "sel_ready", "gath_ps", "xT_act", "xT_vec", "scat_ps", "scat_sb", "gate_ps",
                 "silu_ready", "up_ps", "hid_ready", "hidT_ps", "hidT_sb", "down_ps", "down_act", "down_vec",
                 "scattered")
        first_early_in, second_early_in, third_early_in, third_early_in_sp = map(
            sem, ("first_early_in", "second_early_in", "third_early_in", "third_early_in_sp"))
        w_in_first = sem("w_in_first_half")
        gain_ps, gain_ready = sem("gain_ps"), sem("gain_ready")
        x_added, copied_act = sem("x_added"), sem("copied_act")
        main_s = {n: sem("m_" + n) for n in names}
        more_s = {n: sem("o_" + n) for n in names}
        next_ranks = sem("next_ranks")

        w_in = a["w_in"][0].rearrange("(i p c) n -> i p (c n)", i=W_IN_UNITS, c=2)
        w_out = a["w_out"][0].rearrange("(i c p) n -> i p c n", i=W_OUT_UNITS, c=4)
        w_ple_gate = a["w_ple_gate"][0].rearrange("(j i p c) n -> j p i (c n)", j=2, i=2, c=2)
        w_ple = a["w_ple_proj"][0].rearrange("(c p) n -> p c n", p=P)
        w_gate, w_up = (a[n][0].rearrange("g (q e) (i p c) f -> (g q) i p e (c f)", e=QUAD, p=P, c=2)
                        for n in ("w_gate", "w_up"))
        w_down = a["w_down"][0].rearrange("g (q e) (i p) n -> (g q) i p e n", e=QUAD, p=P)
        x_dram = a["x"][0].rearrange("(t p) n -> t p n", p=P)
        out_dram = out[0].rearrange("(t p) n -> t p n", p=P)
        p_dram = a["p"][0, 0].rearrange("(t p) n -> p t n", p=P)

        def ring_position(u, first_quad):
            return FIRST_EXPERT_UNIT + u + (sum(early > u for early in EARLY) if first_quad else 0)

        def load_early(queue, which, experts, arrived):
            kind, part = divmod(EARLY[which], 4)
            for e in experts:
                places = early_place[which][e]
                n = 1024 // len(places)
                for i, place in enumerate(places):
                    queue.dma_start(place, (w_gate, w_up)[kind][0, part][:, e, n * i:n * i + n]).then_inc(arrived, 16)

        def broadcast(row):
            return row.rearrange("(o n) -> o n", o=1).broadcast_to([P, row.shape[0]])

        def unit(slot):
            return ring[:, slot, :]

        def expert_unit(slot):
            return unit(slot).rearrange("p (e n) -> p e n", e=QUAD)

        def squares(which, t):
            return 4 * which + 2 * t - (2 if which else 0)

        def sum_column(which, t, part):
            return 2 if part == 2 else 4 * which + 2 * t + part

        def half_of(v, t, half):
            return v[:, t, 512 * half:512 * half + 512]

        block = ctx.enter_context(nc.Block())

        @block.sync
        def _(sp):
            for t in range(TILES):
                sp.dma_start(x_sb[:, t, :], x_dram[t]).then_inc(x_in[t], 16)
            sp.dma_start(ident, a["consts"][:, 0:P]).then_inc(ident_in, 16)
            with nc.allow_non_contiguous_dma(reason="512 pairs of values"):
                sp.dma_start(gains[:, 0, :].rearrange("p (i c) -> p i c", c=2),
                             a["g_mix"][0].rearrange("(i p c) -> p i c", i=4, c=2)).then_inc(gains_in, 16)
            sp.sem_inc(ring_free, RING)

            def load_w_in(i):
                sp.dma_start(unit(i), w_in[i]).then_inc(slot_in[i], 16)

            sp.dma_start(unit(0)[:, 0:2048], w_in[0][:, 0:2048]).then_inc(w_in_first, 16)
            sp.dma_start(unit(0)[:, 2048:], w_in[0][:, 2048:]).then_inc(slot_in[0], 16)
            sp.dma_start(consts[:, P:], a["consts"][:, P:C_KEPT]).then_inc(consts_in, 16)
            sp.dma_start(v_area[0:BUCKETS, 0:SEQ], a["consts"][0:BUCKETS, C_KEPT:]).then_inc(bucket_in, 16)
            sp.dma_start(rel_bias[:, :], a["rel_bias"]).then_inc(bucket_in, 16)
            for i in range(1, W_IN_UNITS):
                load_w_in(i)
            sp.dma_start(w_pool[:, :, :], a["w_pool"][0].rearrange("g c d -> c g d")).then_inc(small_in, 16)
            with nc.allow_non_contiguous_dma(reason="single values, a few hundred"):
                sp.dma_start(pool_scale[:, :], a["pool_scale"][0].rearrange("(g d) -> d g", d=P)).then_inc(small_in, 16)
                sp.dma_start(r1_sb, a["w_r1"][0].rearrange("(i p c) g -> p i c g", i=4, c=2)).then_inc(route_in, 16)
                for g in range(GROUPS):
                    sp.dma_start(r2_sb[:, g, :, :], a["w_r2"][0, g].rearrange("(i p c) e -> p i (c e)", i=4, c=2)
                                 ).then_inc(route_in, 16)
                sp.dma_start(router_bias[:, 0:GROUPS], broadcast(a["b_r1"][0])).then_inc(route_in, 16)
                sp.dma_start(router_bias[:, GROUPS:], broadcast(a["b_r2"][0].rearrange("g e -> (g e)"))
                             ).then_inc(route_in, 16)
                for which, name in ((1, "g_ffn"), (2, "g_ple")):
                    sp.dma_start(gains[:, which, :].rearrange("p (i c) -> p i c", c=2),
                                 a[name][0].rearrange("(i p c) -> p i c", i=4, c=2)).then_inc(later_gains_in, 16)
            sp.wait_ge(bias_in, 16)
            for i in range(W_OUT_UNITS):
                s = W_IN_UNITS + i
                sp.dma_start(unit(s).rearrange("p (c n) -> p c n", c=4), w_out[1 - i]).then_inc(slot_in[s], 16)

            def load_step(step, quad0, arrived, free, base, units=range(STEP_UNITS), first_quad=False):
                for u in units:
                    q, i = divmod(u, QUAD_UNITS)
                    kind, part = divmod(i, 4)
                    w = (w_gate, w_up, w_down)[kind]
                    position = ring_position(u, first_quad)
                    sp.wait_ge(free, step * STEP_UNITS + position - base + 1)
                    sp.dma_start(expert_unit(position % RING), w[bass.ds(quad0 + q, 1), part][0]
                                 ).then_inc(arrived[position % RING], 16)

            in_ring = [u for u in range(STEP_UNITS) if u not in EARLY]
            load_step(0, 0, slot_in, ring_free, 0, in_ring[:RING], True)
            sp.wait_ge(squared, squares(1, 1) + 2)
            load_early(sp, 1, (0,), second_early_in)
            sp.wait_ge(logitsT_ps, 1)
            load_early(sp, 1, (2,), second_early_in)
            sp.wait_ge(ple_ps, 2 * TILES)
            load_early(sp, 1, (1, 3), second_early_in)
            for t in range(TILES):
                sp.wait_ge(x_added, 2 * t + 2)
                load_early(sp, 2, (t,), third_early_in_sp)
            load_step(0, 0, slot_in, ring_free, 0, in_ring[RING:], True)
            with sp.Fori(1, STEPS) as step:
                load_step(step, step * QUADS_PER_STEP, slot_in, ring_free, 0)

            sp.wait_ge(routed, 1)
            with sp.If(sp.value_load(most_int[0:1, 0:1], min_val=0, max_val=SEQ) > SLOTS):
                sp.wait_ge(ring_free, RING + FIRST_EXPERT_UNIT + EXPERT_UNITS)
                sp.sem_inc(more_free, RING)
                with sp.Fori(0, PASSES - 1) as again:
                    with sp.Fori(0, STEPS) as step:
                        load_step(again * STEPS + step, step * QUADS_PER_STEP, more_in, more_free, FIRST_EXPERT_UNIT)
                sp.wait_ge(more_free, RING + (PASSES - 1) * EXPERT_UNITS)
            for i in range(2):
                n = FIRST_EXPERT_UNIT + EXPERT_UNITS + i
                sp.wait_ge(ring_free, n + 1)
                sp.dma_start(unit(n % RING).rearrange("p (i n) -> p i n", i=2), w_ple_gate[i]
                             ).then_inc(slot_in[n % RING], 16)
            for t in range(TILES):
                for half in range(2):
                    sp.wait_ge(*((final_out_act, 1) if (t, half) == (1, 0) else (final_out, min(2 * t + half + 1, 3))))
                    sp.dma_start(out_dram[t][:, 512 * half:512 * half + 512], half_of(h_sb, t, half)
                                 ).then_inc(out_done, 16)
            sp.wait_ge(out_done, 16 * 2 * TILES)

        @block.scalar
        def _(act):
            warmed = [0]

            def load_table(func):
                i = warmed[0]
                warmed[0] += 1
                act.activation(warm[:, i:i + 1], eps[:, 0:1], func)

            def square(which, t, part, source, ready, at):
                act.wait_ge(ready, at)
                n = squares(which, t) + part
                if n:
                    act.wait_ge(squared, n)
                column = sum_column(which, t, part)
                act.activation(scratch[:, 0:source.shape[1]], source, ACT.Square,
                               accum_out=sum_sq[:, column:column + 1]).then_inc(squared, 1)

            def root_of(which, t):
                c = 2 * which + t
                if (which, t) == (0, 1):
                    act.wait_ge(squared_vec, 1)
                    part = eps[:, 0:1]
                else:
                    extra = int((which, t) == (3, 1))
                    act.wait_ge(squared, squares(which, t) + 2 + extra)
                    act.wait_ge(based, max(c, 1) + extra)
                    part = base[:, c:c + 1]
                column = sum_column(which, t, 2 if (which, t) == (3, 1) else 1)
                act.activation(root[:, c:c + 1], sum_sq[:, column:column + 1], ACT.Sqrt, scale=1.0 / D,
                               bias=part).then_inc(rooted, 1)

            def by_gain(which, dest, bank, first_chunk=0):
                for c in range(4):
                    last = act.activation(dest[:, c, :], psum[:, bank, P * c:P * c + P], ACT.Copy,
                                          scale=gains[:, which, first_chunk + c:first_chunk + c + 1])
                return last

            def turned_out(which, t, bank, dest):
                act.wait_ge(turned_ps, 4 * which + 2 * t + 1)
                by_gain(which, dest[:, 0:4, t * P:(t + 1) * P], bank).then_inc(turned_act, 1)

            act.wait_ge(vec, 1)
            load_table(ACT.Sqrt)
            for half in range(2):
                square(0, 0, half, half_of(x_sb, 0, half), x_in[0], 16)
            for t in range(TILES):
                root_of(0, t)
            act.wait_ge(inverted, 2)
            act.activation(h_sb[:, 1, :], x_sb[:, 1, :], ACT.Copy, scale=rstd[:, 1:2]).then_inc(scaled[1], 1)
            act.wait_ge(gains_in, 16)
            for t in range(TILES):
                turned_out(0, t, 2 * t, hT)
            load_table(ACT.Exp)

            for b in range(2):
                act.wait_ge(z_ps, b + 1)
                act.copy(u_pad[:, 2 * b:2 * b + 2, PAD:], psum[:, 4 + b, :].rearrange("p (c t) -> p c t", c=2)
                         ).then_inc(z_act, 1)
            for b in range(2):
                act.wait_ge(z_ps, 2 * b + 4)
                act.copy(kT[:, 2 * b:2 * b + 2, :], psum[:, 2 + b, :].rearrange("p (c t) -> p c t", c=2)
                         ).then_inc(z_act, 1)

            def exponents(h):
                act.wait_ge(scored, h + 1)
                if h >= 2:
                    act.wait_ge(probs_ps, h - 1)
                for t in range(TILES):
                    lo, hi = (0, 128) if t == 0 else (128, 384)
                    act.activation(probs[h % 2][:, lo:hi], scores[h % 2][:, lo:hi], ACT.Exp,
                                   bias=neg_max[:, h, t:t + 1], accum_out=row_sum[:, t, h:h + 1]).then_inc(exped, 1)

            def head_pair_out(pair):
                act.wait_ge(attnT_ps, pair + 1)
                act.copy(mixT[:, pair, :], psum[:, 7, 256:512]).then_inc(attnT_sb, 1)

            exponents(0)
            exponents(1)
            act.wait_ge(z_ps, 8)
            act.copy(v_sb[:, 1, :], psum[:, 7, :]).then_inc(z_act, 1)
            for h in range(HEADS):
                if 2 <= h + 1 < HEADS:
                    exponents(h + 1)
                act.wait_ge(probs_ps, h + 1)
                if h >= 2:
                    act.wait_ge(attn_ps, h - 1)
                act.copy(probsT[h % 2], psum[:, 6, 0:384]).then_inc(probs_sb, 1)
                if h % 2 == 0 and h >= 2:
                    head_pair_out(h // 2 - 1)
            load_table(ACT.Sqrt)
            head_pair_out(HEADS // 2 - 1)
            act.wait_ge(attn_ps, HEADS)
            act.wait_ge(pT_ps, 1)
            act.copy(pT, psum[:, 6, :].rearrange("p (c t) -> p c t", c=2)).then_inc(pT_sb, 1)

            def ple_out(t, half):
                act.wait_ge(ple_ps, 2 * t + half + 1)
                act.copy(ple[t][:, 512 * half:512 * half + 512], psum[:, PLE_BANKS[t][half], :]).then_inc(ple_sb, 1)

            act.wait_ge(later_gains_in, 32)
            for t in range(TILES):
                if t:
                    for tile in range(TILES):
                        turned_out(1, tile, 4 + 2 * tile, hT)
                for half in range(2):
                    square(1, t, half, half_of(h_sb, t, half), summed, 2 * t + half + 1)
                root_of(1, t)
            load_table(ACT.Exp)
            for t in range(TILES):
                act.wait_ge(turned_ps, 4 + 2 * t + 2)
                act.wait_ge(inverted, 2 + t + 1)
                act.activation(h_sb[:, t, :], h_sb[:, t, :], ACT.Copy, scale=rstd[:, 2 + t:3 + t]).then_inc(normed, 1)
            ple_out(0, 0)
            ple_out(0, 1)
            act.wait_ge(exp_in, 1)
            act.activation(shifted_exp, shifted, ACT.Exp).then_inc(exp_out, 1)
            ple_out(1, 0)
            ple_out(1, 1)
            act.wait_ge(exp_in, 2)
            act.activation(tiny[:, 6, :], tiny[:, 5, :], ACT.Exp).then_inc(exp_out, 1)
            load_table(ACT.Silu)

            def moe_step(step, s, first_quad=False):
                for q in range(QUADS_PER_STEP):
                    n = step * QUADS_PER_STEP + q
                    act.wait_ge(s["gath_ps"], n * 2 + 1)
                    by_gain(1, xT[:, 0:4, :], 6).then_inc(s["xT_act"], 1)
                    act.wait_ge(s["gate_ps"], n + 1)
                    act.activation(silu, psum[:, 4, :], ACT.Silu).then_inc(s["silu_ready"], 1)
                    if first_quad and q == 1:
                        act.wait_ge(gain_ps, 1)
                        act.copy(g_final[:, :].rearrange("p (b n) -> p b n", b=2), psum[:, 6:8, :]
                                 ).then_inc(gain_ready, 1)
                    act.wait_ge(s["hidT_ps"], n + 1)
                    act.copy(hiddenT[:, :, :], psum[:, 4, :].rearrange("p (c s) -> p c s", c=4)
                             ).then_inc(s["hidT_sb"], 1)
                    act.wait_ge(s["down_ps"], n + 1)
                    act.copy(down_sb[:, 0:512], psum[:, 6, :]).then_inc(s["down_act"], 1)

            moe_step(0, main_s, first_quad=True)
            with act.Fori(1, STEPS) as step:
                moe_step(step, main_s)
            act.wait_ge(routed, 1)
            with act.If(act.value_load(most_int[0:1, 0:1], min_val=0, max_val=SEQ) > SLOTS):
                with act.Fori(0, PASSES - 1) as again:
                    with act.Fori(0, STEPS) as step:
                        moe_step(again * STEPS + step, more_s)
                act.wait_ge(more_s["scattered"], (PASSES - 1) * 2 * EXPERTS // QUAD)
                act.nop()
            load_table(ACT.Sqrt)
            for t in range(TILES):
                act.wait_ge(main_s["scattered"], 2 * EXPERTS // QUAD - 1 + t)
                act.copy(half_of(x_sb, t, 1), psum[:, 2 * t + 1, :]).then_inc(copied_act, 1)
            for t in range(TILES):
                act.wait_ge(turned_ps, 8 + 2 * t + 2)
                by_gain(2, gateT[:, 4:8, t * P:(t + 1) * P], 5 + 2 * t, first_chunk=4).then_inc(turned_act, 1)
            for t in range(TILES):
                for half in range(2):
                    square(2, t, half, half_of(x_sb, t, half), *((summed, 4 + t + 1), (copied_act, t + 1))[half])
                root_of(2, t)
            load_table(ACT.Sigmoid)
            for n, (t, lo, hi, bank) in enumerate(PIECES):
                act.wait_ge(open_ps, n + 1)
                act.wait_ge(inverted, 4 + t + 1)
                act.activation(h_sb[:, t, lo:hi], psum[:, bank, 0:hi - lo],
                               ACT.Sigmoid, scale=rstd[:, 4 + t:5 + t]).then_inc(opened, 1)
                if hi == D:
                    load_table(ACT.Sqrt)
                square(3, t, n - 2 * t, x_sb[:, t, lo:hi], final_x, n + 1)
                if hi == D:
                    root_of(3, t)
                    if t == 0:
                        load_table(ACT.Sigmoid)
            act.wait_ge(gained, 1)
            act.wait_ge(inverted, 8)
            act.activation(half_of(h_sb, 1, 0), half_of(h_sb, 1, 0), ACT.Copy, scale=rstd[:, 7:8]
                           ).then_inc(final_out_act, 1)

        @block.gpsimd
        def _(pool):
            pool.memset(pool_area[:, 0:3 * width].rearrange("p (g t) -> p g t", g=3 * POOL_GROUPS)[:, :, 0:PAD], 0.0
                        ).then_inc(padded, 1)
            pool.wait_ge(bias_row_ready, 2)
            pool.dma_start(bias_dram[:, :], bias_row).then_inc(bias_out, 16)
            pool.wait_ge(bias_out, 16)
            skewed = bass.AP(tensor=bias_dram.tensor, offset=0, ap=[[1, P], [BIAS_ROW, HEADS], [1, SEQ]])
            pool.dma_start(bias_of, skewed).then_inc(bias_in, 16)
            pool.dma_start(p_sb, p_dram).then_inc(p_in, 16)
            pool.wait_ge(route_in, 16 * (3 + GROUPS))
            pool.tensor_copy(router[:, :, 0:GROUPS], r1_sb.rearrange("p i c g -> p (i c) g")
                             ).then_inc(router_ready, 1)
            for g in range(GROUPS):
                lo = GROUPS + g * GROUP_EXPERTS
                pool.tensor_copy(router[:, :, lo:lo + GROUP_EXPERTS],
                                 r2_sb[:, g, :, :].rearrange("p i (c e) -> p (i c) e", c=2)).then_inc(router_ready, 1)
            pool.wait_ge(consts_in, 16)
            pool.wait_ge(padded, 1)
            pool.wait_ge(z_act, 2)
            source, dest, n = u_pad, sum_a, 0
            for stage, w in enumerate(POOL_WINDOWS):
                half = w // 2
                pool.tensor_tensor(dest[:, stage:, PAD:], source[:, stage:, PAD:],
                                   source[:, stage:, PAD - half:PAD + SEQ - half], ALU.add).then_inc(pool_step, 1)
                n += 1
                pool.wait_ge(pool_step, n)
                sums = dest[:, stage, PAD:]
                pool.tensor_scalar(sums[:, PAD:], sums[:, PAD:], 1.0 / w, None, ALU.mult).then_inc(pool_step, 1)
                pool.tensor_tensor(sums[:, 0:PAD], sums[:, 0:PAD], edge[:, stage, :], ALU.mult).then_inc(pool_step, 1)
                n += 2
                pool.wait_ge(pool_step, n)
                pool.tensor_tensor(sums, sums, u_pad[:, stage, PAD:], ALU.subtract).then_inc(pooled, 1)
                source, dest = dest, (sum_b if dest is sum_a else sum_a)
            pool.wait_ge(pool_ps, POOL_GROUPS)
            load_early(pool, 0, (0, 1), first_early_in)
            pool.wait_ge(scored, HEADS)
            load_early(pool, 0, (2, 3), first_early_in)
            pool.dma_start(w_ple_sb, w_ple).then_inc(w_ple_in, 16)
            load_early(pool, 2, (2, 3), third_early_in)
            pool.wait_ge(main_s["scattered"], 2)
            pool.dma_start(g_final_row, a["g_final"].rearrange("(o n) -> o n", o=1)).then_inc(gain_row_in, 16)

        @block.vector
        def _(dve):
            steps = [0]

            def done(ins):
                steps[0] += 1
                ins.then_inc(vec, 1)
                dve.wait_ge(vec, steps[0])

            dve.memset(filler, 0.0).then_inc(filler_ready, 1)
            done(dve.memset(eps[:, :], EPS))
            dve.memset(bias_row[:, SEQ:BIAS_ROW], MASKED).then_inc(bias_row_ready, 1)

            def base_of(which, t):
                c = 2 * which + t
                dve.wait_ge(squared, squares(which, t) + 1)
                dve.tensor_scalar(base[:, c:c + 1], sum_sq[:, 2 * c:2 * c + 1], 1.0 / D, EPS, ALU.mult, ALU.add
                                  ).then_inc(based, 1)

            def invert(which, t):
                c = 2 * which + t
                dve.wait_ge(rooted, c + 1)
                dve.reciprocal(rstd[:, c:c + 1], root[:, c:c + 1]).then_inc(inverted, 1)
                dve.wait_ge(inverted, c + 1)
                return rstd[:, c:c + 1]

            def by_gain(which, dest, bank, first_chunk=4):
                return dve.tensor_tensor(
                    dest, psum[:, bank, :].rearrange("p (c s) -> p c s", c=4),
                    gains[:, which, first_chunk:first_chunk + 4].unsqueeze(2).broadcast_to([P, 4, P]), ALU.mult)

            def turned_out(which, t, bank, dest):
                dve.wait_ge(turned_ps, 4 * which + 2 * t + 2)
                by_gain(which, dest[:, 4:8, t * P:(t + 1) * P], bank).then_inc(turned_vec, 1)

            dve.wait_ge(x_in[1], 16)
            dve.tensor_tensor_reduce(h_sb[:, 1, :], x_sb[:, 1, :], x_sb[:, 1, :], 1.0, 0.0, ALU.mult, ALU.add,
                                     sum_sq[:, 3:4]).then_inc(squared_vec, 1)
            base_of(0, 0)
            for t in range(TILES):
                invert(0, t)
                if t == 0:
                    dve.tensor_scalar(h_sb[:, 0, :], x_sb[:, 0, :], rstd[:, 0:1], None, ALU.mult).then_inc(scaled[0], 1)
            dve.wait_ge(gains_in, 16)
            for t in range(TILES):
                turned_out(0, t, 2 * t + 1, hT)
            dve.wait_ge(bias_ps, 1)
            dve.tensor_copy(bias_row[:, 0:SEQ], psum[0:HEADS, 7, 0:SEQ]).then_inc(bias_row_ready, 1)
            for b in range(2):
                dve.wait_ge(z_ps, 2 * b + 3)
                for c in range(2):
                    for t in range(TILES):
                        lo = 256 * c + 128 * t
                        last = dve.tensor_scalar(qT[:, 2 * b + c, P * t:P * t + P],
                                                 psum[:, b, lo:lo + P][:, ::-1], HEAD_DIM ** -0.5, None, ALU.mult)
                last.then_inc(z_vec, 1)

            def biased(h):
                dve.wait_ge(scores_ps, h + 1)
                if h >= 2:
                    dve.wait_ge(exped, 2 * (h - 1))
                for t in range(TILES):
                    lo, hi = (0, 128) if t == 0 else (128, 384)
                    done(dve.tensor_tensor_reduce(scores[h % 2][:, lo:hi], psum[:, 4 + h % 2, lo:hi],
                                                  bias_of[:, h, 256 - (hi - lo):256], 1.0, 3 * MASKED, ALU.add,
                                                  ALU.max, row_max[:, h, t:t + 1]))
                dve.tensor_scalar(neg_max[:, h, :], row_max[:, h, :], -1.0, None, ALU.mult).then_inc(scored, 1)

            dve.wait_ge(bias_in, 16)
            biased(0)
            biased(1)
            dve.wait_ge(z_ps, 7)
            dve.tensor_copy(v_sb[:, 0, :], psum[:, 6, :]).then_inc(z_vec, 1)
            dve.wait_ge(small_in, 32)
            for g in range(POOL_GROUPS):
                dve.wait_ge(pool_ps, 2 * (g // 2) + 2)
                dve.tensor_scalar(mixT[:, 4 + g, :], psum[:, g // 2, 256 * (g % 2):256 * (g % 2) + 256],
                                  pool_scale[:, g:g + 1], None, ALU.mult).then_inc(pool_done, 1)
            for h in range(HEADS):
                if h + 2 < HEADS:
                    biased(h + 2)
                if h % 2:
                    pair = slice(h - 1, h + 1)
                    dve.wait_ge(exped, 2 * (h + 1))
                    done(dve.reciprocal(row_inv[:, :, pair], row_sum[:, :, pair]))
                    dve.wait_ge(attn_ps, h + 1)
                    dve.tensor_tensor(
                        h_sb[:, :, (h - 1) * HEAD_DIM:(h + 1) * HEAD_DIM].rearrange("p t (h d) -> p t h d", h=2),
                        psum[:, 7, 0:256].rearrange("p (t h d) -> p t h d", t=TILES, h=2),
                        row_inv[:, :, pair].unsqueeze(3).broadcast_to([P, TILES, 2, HEAD_DIM]),
                        ALU.mult).then_inc(attn_sb, 1)
            dve.wait_ge(attnT_ps, HEADS // 2)
            dve.wait_ge(pT_ps, 1)
            for t in range(TILES):
                for half in range(2):
                    dve.wait_ge(mix_ps, 2 * t + half + 1)
                    dve.tensor_tensor(half_of(h_sb, t, half), half_of(x_sb, t, half), psum[:, 2 * t + half, :],
                                      ALU.add).then_inc(summed, 1)
            base_of(1, 0)
            dve.wait_ge(later_gains_in, 32)
            for t in range(TILES):
                turned_out(1, t, 5 + 2 * t, hT)
            base_of(1, 1)
            for t in range(TILES):
                invert(1, t)

            def row(i):
                return small[:, i, :, :]

            def spread(v, n):
                return v.unsqueeze(2).broadcast_to([P, TILES, n])

            dve.wait_ge(consts_in, 16)
            dve.wait_ge(route_in, 16 * (3 + GROUPS))
            dve.wait_ge(logitsT_ps, 1)
            dve.tensor_copy(logitsT, psum[0:GROUPS + EXPERTS, 6, 0:SEQ]).then_inc(logitsT_sb, 1)
            dve.wait_ge(logits_ps, 1)
            for t in range(TILES):
                done(dve.scalar_tensor_tensor(out=logits[:, t, 0:GROUPS + EXPERTS],
                                              in0=psum[:, 7, 64 * t:64 * t + GROUPS + EXPERTS],
                                              scalar=rstd[:, 2 + t:3 + t], in1=router_bias[:, :],
                                              op0=ALU.mult, op1=ALU.add))
            group_logits, expert_logits = logits[:, :, 0:GROUPS], logits[:, :, GROUPS:GROUPS + EXPERTS]

            def one_hot(values, n, top, dest, scratch, inverse=False):
                done(dve.tensor_reduce(top, values, AX, ALU.max))
                for t in range(TILES):
                    last = dve.scalar_tensor_tensor(out=dest[:, t, :], in0=values[:, t, :], scalar=top[:, t:t + 1],
                                                    in1=first[:, 0:n], op0=ALU.is_equal, op1=ALU.mult)
                done(last)
                done(dve.tensor_reduce(scratch, dest, AX, ALU.max))
                done(dve.tensor_tensor(dest, dest, spread(scratch, n), ALU.not_equal if inverse else ALU.is_equal))

            top_g, top_1, top_2, scratch_top = (tiny[:, i, :] for i in range(4))
            one_hot(group_logits, GROUPS, top_g, other_group, scratch_top, inverse=True)
            dve.tensor_tensor(shifted, group_logits, spread(top_g, GROUPS), ALU.subtract).then_inc(exp_in, 1)
            kept = row(3)
            for t in range(TILES):
                last = dve.scalar_tensor_tensor(
                    out=kept[:, t, :].rearrange("p (g e) -> p g e", g=GROUPS),
                    in0=other_group[:, t, :].unsqueeze(2).broadcast_to([P, GROUPS, GROUP_EXPERTS]), scalar=MASKED,
                    in1=expert_logits[:, t, :].rearrange("p (g e) -> p g e", g=GROUPS), op0=ALU.mult, op1=ALU.add)
            done(last)
            best, second = row(4), row(5)
            one_hot(kept, EXPERTS, top_1, best, scratch_top)
            done(dve.scalar_tensor_tensor(out=kept, in0=best, scalar=MASKED, in1=kept, op0=ALU.mult, op1=ALU.add))
            one_hot(kept, EXPERTS, top_2, second, scratch_top)
            taken, no_slot = row(6), row(9)
            dve.tensor_tensor(taken, best, second, ALU.add).then_inc(chosen, 1)
            dve.tensor_tensor(tiny[:, 5, :], top_2, top_1, ALU.subtract).then_inc(exp_in, 1)
            dve.wait_ge(chosen, 1)
            done(dve.tensor_scalar(no_slot, taken, -NO_SLOT, NO_SLOT, ALU.mult, ALU.add))
            dve.wait_ge(rank_ps, 1)
            done(dve.tensor_tensor(ranks[:, :, :], psum[:, 7, 0:64].rearrange("p (t e) -> p t e", t=TILES),
                                   no_slot, ALU.add))
            gates = row(7)

            def work_out_gates():
                dve.wait_ge(exp_out, 1)
                done(dve.tensor_reduce(tiny[:, 7, :], shifted_exp, AX, ALU.add))
                done(dve.reciprocal(tiny[:, 8, :], tiny[:, 7, :]))
                dve.wait_ge(exp_out, 2)
                done(dve.tensor_scalar(tiny[:, 9, :], tiny[:, 6, :], 1.0, None, ALU.add))
                done(dve.reciprocal(tiny[:, 10, :], tiny[:, 9, :]))
                done(dve.tensor_tensor(tiny[:, 11, :], tiny[:, 10, :], tiny[:, 8, :], ALU.mult))
                done(dve.tensor_tensor(tiny[:, 12, :], tiny[:, 11, :], tiny[:, 6, :], ALU.mult))
                done(dve.tensor_tensor(gates, best, spread(tiny[:, 11, :], EXPERTS), ALU.mult))
                done(dve.tensor_tensor(row(8), second, spread(tiny[:, 12, :], EXPERTS), ALU.mult))
                done(dve.tensor_tensor(gates, gates, row(8), ALU.add))
                dve.tensor_copy(most_int[:, :], most).then_inc(routed, 1)

            done(dve.tensor_reduce(most, psum[:, 7, 64:96], AX, ALU.max))

            def moe_step(step, quad0, s, moved_on=None, first_quad=False):
                if moved_on is not None:
                    dve.wait_ge(next_ranks, moved_on)
                for q in range(QUADS_PER_STEP):
                    n = step * QUADS_PER_STEP + q
                    e0 = (quad0 + q) * QUAD

                    def of_quad(v):
                        return v[:, :, bass.ds(e0, QUAD)].unsqueeze(3).broadcast_to([P, TILES, QUAD, SLOTS])

                    dve.tensor_tensor(select, of_quad(ranks[:, :, :]),
                                      slot_no.unsqueeze(1).unsqueeze(1).broadcast_to([P, TILES, QUAD, SLOTS]),
                                      ALU.is_equal).then_inc(s["selected"], 1)
                    dve.wait_ge(s["selected"], n + 1)
                    if first_quad and q == 0:
                        work_out_gates()
                    dve.tensor_tensor(weighted, select, of_quad(gates), ALU.mult).then_inc(s["sel_ready"], 1)
                    dve.wait_ge(s["gath_ps"], n * 2 + 2)
                    by_gain(1, xT[:, 4:8, :], 7).then_inc(s["xT_vec"], 1)
                    dve.wait_ge(s["scat_ps"], n + 1)
                    dve.tensor_copy(scatterT, psum[:, 5, 0:256]).then_inc(s["scat_sb"], 1)
                    dve.wait_ge(s["silu_ready"], n + 1)
                    dve.wait_ge(s["up_ps"], n + 1)
                    dve.tensor_tensor(hidden, silu, psum[:, 5, :], ALU.mult).then_inc(s["hid_ready"], 1)
                    dve.wait_ge(s["down_ps"], n + 1)
                    dve.tensor_copy(down_sb[:, 512:1024], psum[:, 7, :]).then_inc(s["down_vec"], 1)

            moe_step(0, 0, main_s, first_quad=True)
            with dve.Fori(1, STEPS) as step:
                moe_step(step, step * QUADS_PER_STEP, main_s)
            dve.wait_ge(routed, 1)
            with dve.If(dve.value_load(most_int[0:1, 0:1], min_val=0, max_val=SEQ) > SLOTS):
                with dve.Fori(0, PASSES - 1) as again:
                    dve.tensor_scalar(ranks[:, :, :], ranks[:, :, :], float(-SLOTS), None, ALU.add
                                      ).then_inc(next_ranks, 1)
                    with dve.Fori(0, STEPS) as step:
                        moe_step(again * STEPS + step, step * QUADS_PER_STEP, more_s, again + 1)
                dve.wait_ge(more_s["scattered"], (PASSES - 1) * 2 * EXPERTS // QUAD)
                dve.nop()

            for t in range(TILES):
                dve.wait_ge(main_s["scattered"], 2 * EXPERTS // QUAD - 1 + t)
                dve.tensor_copy(half_of(x_sb, t, 0), psum[:, 2 * t, :]).then_inc(summed, 1)
            for t in range(TILES):
                dve.wait_ge(turned_ps, 8 + 2 * t + 1)
                by_gain(2, gateT[:, 0:4, t * P:(t + 1) * P], 4 + 2 * t, first_chunk=0).then_inc(turned_vec, 1)
            for t in range(TILES):
                base_of(2, t)
            for t in range(TILES):
                invert(2, t)
            dve.wait_ge(gain_ready, 1)
            dve.wait_ge(ple_sb, 2 * TILES)
            for n, (t, lo, hi, _) in enumerate(PIECES):
                gate, x_part = h_sb[:, t, lo:hi], x_sb[:, t, lo:hi]
                dve.wait_ge(opened, n + 1)
                done(dve.tensor_tensor(gate, gate, ple[t][:, lo:hi], ALU.mult))
                dve.tensor_tensor(x_part, x_part, gate, ALU.add).then_inc(final_x, 1)
                if lo == 0:
                    base_of(3, t)
                    if t == 1:
                        dve.wait_ge(final_x, n + 1)
                        dve.tensor_tensor(gate, x_part, g_final[:, lo:hi], ALU.mult).then_inc(gained, 1)
                elif hi < D:
                    dve.wait_ge(squared, squares(3, 1) + 2)
                    dve.wait_ge(based, 7)
                    column = sum_column(3, 1, 1)
                    dve.scalar_tensor_tensor(out=base[:, 7:8], in0=sum_sq[:, column:column + 1], scalar=1.0 / D,
                                             in1=base[:, 7:8], op0=ALU.mult, op1=ALU.add).then_inc(based, 1)
                else:
                    scale = invert(3, t)
                    for half in range(t, 2):
                        dve.scalar_tensor_tensor(out=half_of(h_sb, t, half), in0=half_of(x_sb, t, half), scalar=scale,
                                                 in1=g_final[:, 512 * half:512 * half + 512], op0=ALU.mult,
                                                 op1=ALU.mult).then_inc(final_out, 1)

        @block.tensor
        def _(pe):
            def pairs(v, t, c):
                i, c2 = divmod(c, 2)
                return v[:, t, 256 * i + c2:256 * i + 256:2]

            def turn(which, t, source):
                for c in range(8):
                    if c % 4 == 0 and which == 1:
                        pe.wait_ge(summed, 2 * t + c // 4 + 1)
                    elif c % 4 == 0:
                        pe.wait_ge(*((summed, 4 + t + 1), (copied_act, t + 1))[c // 4])
                    last = pe.transpose(psum[:, 4 + 2 * t + c // 4, P * (c % 4):P * (c % 4) + P],
                                        pairs(source, t, c), ident)
                    if (which, t, c) == (1, 0, 0):
                        last.then_inc(ring_free, 1)
                    if c % 4 == 3:
                        last.then_inc(turned_ps, 1)

            def stay_warm(bank, n):
                for _ in range(n):
                    pe.matmul(psum[:, bank, 0:P], filler, filler, start=True, stop=True)

            pe.wait_ge(filler_ready, 1)
            stay_warm(7, 22)
            pe.wait_ge(ident_in, 16)
            for t in range(TILES):
                pe.wait_ge(scaled[t], 1)
                for c in range(8):
                    last = pe.transpose(psum[:, 2 * t + c // 4, P * (c % 4):P * (c % 4) + P], pairs(h_sb, t, c), ident)
                    if c % 4 == 3:
                        last.then_inc(turned_ps, 1)
            chunk_bank = {**{c: c // 2 for c in range(8)}, **{12 + g: 4 + g // 2 for g in range(4)}}
            order = [12, 13, 14, 15, 0, 1, 4, 5, 2, 3, 6, 7]
            w = [unit(i).rearrange("p (c n) -> p c n", c=2) for i in range(W_IN_UNITS)]

            def project(c, m):
                half = SEQ * (m % 2)
                return pe.matmul(psum[:, chunk_bank[m], half:half + SEQ], w[c // 2][:, c % 2, P * m:P * m + P],
                                 hT[:, c, :], start=(c == 0 and m % 2 == 0), stop=(c == 7), skip_group_check=True)

            def project_v(c, t):
                return pe.matmul(psum[:, 6 + t, :], hT[:, c, t * P:(t + 1) * P], w[c // 2][:, c % 2, 1024:1536],
                                 start=(c == 0), stop=(c == 7), skip_group_check=True)

            pe.wait_ge(turned_act, 2)
            pe.wait_ge(turned_vec, 2)
            pe.wait_ge(w_in_first, 16)
            for c in range(6):
                if c > 0 and c % 2 == 0 or c == 1:
                    pe.wait_ge(slot_in[c // 2], 16)
                for m in order:
                    project(c, m)
                if c == 0:
                    pe.wait_ge(bucket_in, 32)
                    pe.matmul(psum[0:HEADS, 7, 0:SEQ], rel_bias[:, :], bucket_of, start=True, stop=True
                              ).then_inc(bias_ps, 1)
            pe.wait_ge(slot_in[3], 16)
            for i in range(0, 12, 2):
                for m in order[i:i + 2]:
                    for c in (6, 7):
                        last = project(c, m)
                last.then_inc(z_ps, 1)

            def score(h):
                r = HEAD_DIM * (h % 2)
                q_h, k_h = (v[r:r + HEAD_DIM, h // 2, :] for v in (qT, kT))
                if h >= 2:
                    pe.wait_ge(scored, h - 1)
                pe.matmul(psum[:, 4 + h % 2, 0:128], q_h[:, 0:P], k_h[:, 0:P], start=True, stop=True)
                pe.matmul(psum[:, 4 + h % 2, 128:384], q_h[:, P:], k_h, start=True, stop=True).then_inc(scores_ps, 1)

            def mix(c, t, first_one, last_one):
                w_c = unit(W_IN_UNITS + 1 - c // 4).rearrange("p (c n) -> p c n", c=4)[:, c % 4, :]
                for half in range(2):
                    last = pe.matmul(psum[:, 2 * t + half, :], mixT[:, c, t * P:(t + 1) * P],
                                     w_c[:, 512 * half:512 * half + 512], start=first_one, stop=last_one,
                                     skip_group_check=True)
                    if last_one:
                        last.then_inc(mix_ps, 1)

            def turn_probs(h):
                pe.wait_ge(exped, 2 * (h + 1))
                if h >= 1:
                    pe.wait_ge(probs_sb, h)
                for i in range(3):
                    last = pe.transpose(psum[:, 6, P * i:P * i + P], probs[h % 2][:, P * i:P * i + P], ident)
                    if h + i == 0:
                        last.then_inc(ring_free, 1)
                last.then_inc(probs_ps, 1)

            def turn_pair(pair):
                pe.wait_ge(attn_sb, pair + 1)
                for t in range(TILES):
                    last = pe.transpose(psum[:, 7, 256 + P * t:256 + P * t + P],
                                        h_sb[:, t, pair * P:(pair + 1) * P], flip)
                last.then_inc(attnT_ps, 1)

            def attend(h):
                pe.wait_ge(probs_sb, h + 1)
                if h % 2 == 0 and h >= 2:
                    pe.wait_ge(attnT_sb, h // 2)
                o = psum[:, 7, 0:256].rearrange("p (t h d) -> p t h d", t=TILES, h=2)
                values = v_sb[:, :, h * HEAD_DIM:(h + 1) * HEAD_DIM]
                head_first = pe.matmul(o[:, 0, h % 2, :], probsT[h % 2][:, 0:P], values[:, 0, :], start=True, stop=True)
                if h == 5:
                    head_first.then_inc(ring_free, 1)
                pe.matmul(o[:, 1, h % 2, :], probsT[h % 2][:, P:2 * P], values[:, 0, :], start=True, stop=False)
                pe.matmul(o[:, 1, h % 2, :], probsT[h % 2][:, 2 * P:], values[:, 1, :], start=False, stop=True
                          ).then_inc(attn_ps, 1)

            pe.wait_ge(bias_row_ready, 2)
            for t in range(TILES):
                project_v(0, t)
            pe.wait_ge(z_vec, 2)
            pe.wait_ge(z_act, 4)
            score(0)
            score(1)
            for c in range(1, 8):
                for t in range(TILES):
                    last = project_v(c, t)
                    if t == 0 and c % 2 == 0 and c > 0:
                        last.then_inc(ring_free, 1)
                    if c == 7:
                        last.then_inc(z_ps, 1)
            pe.wait_ge(small_in, 32)
            for g in range(POOL_GROUPS):
                pe.wait_ge(pooled, g + 1)
                pe.matmul(psum[:, g // 2, 256 * (g % 2):256 * (g % 2) + 256], w_pool[:, g, :],
                          (sum_a, sum_b)[g % 2][:, g, PAD:], start=True, stop=True).then_inc(pool_ps, 1)
            pe.wait_ge(slot_in[4], 16)
            pe.wait_ge(consts_in, 16)
            pe.wait_ge(z_vec, 3)
            for h in range(HEADS):
                turn_probs(h)
                if h % 2 == 0 and h >= 2:
                    turn_pair(h // 2 - 1)
                if h + 2 < HEADS:
                    score(h + 2)
                if h == 0:
                    pe.wait_ge(z_act, 5)
                    pe.wait_ge(pool_done, POOL_GROUPS)
                for c, t in MIX_BETWEEN[h]:
                    if c < 4:
                        pe.wait_ge(slot_in[5], 16)
                        pe.wait_ge(attnT_sb, c + 1)
                    mix(c, t, (c, h) == (4, 0), False)
                attend(h)
            pe.wait_ge(attnT_sb, 3)
            mix(2, 0, False, False)
            turn_pair(3)
            mix(2, 1, False, False)
            pe.wait_ge(p_in, 16)
            pe.wait_ge(probs_sb, HEADS)
            for c in range(2):
                for t in range(TILES):
                    last = pe.transpose(psum[:, 6, SEQ * c + P * t:SEQ * c + P * t + P],
                                        p_sb[:, t, c * P:(c + 1) * P], ident)
            last.then_inc(pT_ps, 1)
            pe.wait_ge(attnT_sb, 4)
            for t in range(TILES):
                mix(3, t, False, True)

            for t in range(TILES):
                if t:
                    pe.wait_ge(pT_sb, 1)
                    pe.wait_ge(attnT_sb, 4)
                turn(1, t, h_sb)
            def embed(t, half, c):
                last = pe.matmul(psum[:, PLE_BANKS[t][half], :], pT[:, c, t * P:(t + 1) * P],
                                 w_ple_sb[:, c, 512 * half:512 * half + 512], start=(c == 0), stop=(c == 1))
                if c == 1:
                    last.then_inc(ple_ps, 1)

            pe.wait_ge(w_ple_in, 16)
            pe.wait_ge(turned_vec, 3)
            embed(0, 0, 0)
            embed(0, 0, 1)
            pe.wait_ge(router_ready, 1 + GROUPS)
            pe.wait_ge(turned_act, 4)
            pe.wait_ge(turned_vec, 4)
            for c in range(8):
                last = pe.matmul(psum[0:GROUPS + EXPERTS, 6, 0:SEQ], router[:, c, :], hT[:, c, :],
                                 start=(c == 0), stop=(c == 7))
            last.then_inc(logitsT_ps, 1)
            embed(0, 1, 0)
            pe.wait_ge(logitsT_sb, 1)
            for t in range(TILES):
                last = pe.transpose(psum[:, 7, 64 * t:64 * t + GROUPS + EXPERTS], logitsT[:, t * P:(t + 1) * P],
                                    ident[0:GROUPS + EXPERTS, 0:GROUPS + EXPERTS])
            last.then_inc(logits_ps, 1)
            embed(0, 1, 1)
            embed(1, 0, 0)
            embed(1, 0, 1)
            pe.wait_ge(ple_sb, 1)
            embed(1, 1, 0)
            embed(1, 1, 1)
            def add_x(t, half):
                pe.matmul(psum[:, 2 * t + half, :], ident, half_of(x_sb, t, half), start=False, stop=False,
                          skip_group_check=True).then_inc(x_added, 1)

            add_x(0, 0)
            pe.wait_ge(chosen, 1)
            taken = small[:, 6, :, :]
            pe.matmul(psum[:, 7, 0:32], earlier, taken[:, 0, :], start=True, stop=True)
            pe.matmul(psum[:, 7, 32:64], earlier, taken[:, 1, :], start=True, stop=False)
            pe.matmul(psum[:, 7, 32:64], ones, taken[:, 0, :], start=False, stop=True)
            pe.matmul(psum[:, 7, 64:96], ones, taken[:, 0, :], start=True, stop=False)
            pe.matmul(psum[:, 7, 64:96], ones, taken[:, 1, :], start=False, stop=True).then_inc(rank_ps, 1)
            add_x(0, 1)
            pe.wait_ge(ple_sb, 2 * TILES)

            def moe_step(step, s, arrived, free, base, first_quad=False):
                def unit_in(u):
                    if first_quad and u in EARLY:
                        which = EARLY.index(u)
                        for arrived_early, n_parts in (((first_early_in, 4),), ((second_early_in, 4),),
                                                       ((third_early_in, 3), (third_early_in_sp, 2)))[which]:
                            pe.wait_ge(arrived_early, 16 * n_parts)
                        return [[v[:, lo:lo + 512] for v in places for lo in range(0, v.shape[1], 512)]
                                for places in early_place[which]]
                    position = ring_position(u, first_quad)
                    pe.wait_ge(arrived[position % RING],
                               step * (16 * STEP_USES) + 16 * ((position - base) // RING + 1))
                    return [[expert_unit(position % RING)[:, e, lo:lo + 512] for lo in (0, 512)]
                            for e in range(QUAD)]

                def strips(bank, lhsT, w_u, part, start, stop, used_before):
                    for e in range(QUAD):
                        last = pe.matmul(psum[SLOTS * e:SLOTS * e + SLOTS, bank, :],
                                         lhsT[:, SLOTS * e:SLOTS * e + SLOTS], w_u[e][part],
                                         start=start, stop=stop, skip_group_check=True)
                        if used_before and e == 0:
                            last.then_inc(free, 1)
                    return last

                def gather(half, first_unit_used=False):
                    for c in range(4 * half, 4 * half + 4):
                        for t in range(TILES):
                            last = pe.matmul(psum[:, 6 + half, P * (c % 4):P * (c % 4) + P], pairs(h_sb, t, c),
                                             select[:, t, :, :], start=(t == 0), stop=(t == 1))
                            if first_unit_used and c % 4 + t == 0:
                                last.then_inc(free, 1)
                    return last

                for q in range(QUADS_PER_STEP):
                    n = step * QUADS_PER_STEP + q
                    pe.wait_ge(s["selected"], n + 1)
                    gather(0).then_inc(s["gath_ps"], 1)
                    if first_quad and q == 0:
                        add_x(1, 0)
                        add_x(1, 1)
                    pe.wait_ge(s["xT_act"], n + 1)
                    for kind, name in enumerate(("gate_ps", "up_ps")):
                        for i in range(4):
                            if (kind, i) == (0, 1):
                                gather(1, first_unit_used=True).then_inc(s["gath_ps"], 1)
                            if (kind, i) == (0, 2):
                                pe.wait_ge(s["sel_ready"], n + 1)
                                for t in range(TILES):
                                    last = pe.matmul(psum[:, 5, P * t:P * t + P], weighted[:, t, :, :], ident,
                                                     start=True, stop=True)
                                last.then_inc(s["scat_ps"], 1)
                                pe.wait_ge(s["xT_vec"], n + 1)
                            if (kind, i) == (1, 0):
                                pe.wait_ge(s["scat_sb"], n + 1)
                            u = q * QUAD_UNITS + 4 * kind + i
                            w_u = unit_in(u)
                            gives_back = 4 * kind + i > 1 and not (first_quad and u - 1 in EARLY)
                            for c2 in range(2):
                                last = strips(4 + kind, xT[:, 2 * i + c2, :], w_u, c2, i + c2 == 0,
                                              i == 3 and c2 == 1, gives_back and c2 == 0)
                        last.then_inc(s[name], 1)
                    if first_quad and q == 1:
                        pe.wait_ge(gain_row_in, 16)
                        for half in range(2):
                            last = pe.matmul(psum[:, 6 + half, :], ones[0:1, :],
                                             g_final_row[:, 512 * half:512 * half + 512], start=True, stop=True)
                        last.then_inc(gain_ps, 1)
                        pe.wait_ge(gain_ready, 1)
                    pe.wait_ge(s["hid_ready"], n + 1)
                    for c in range(4):
                        last = pe.transpose(psum[:, 4, P * c:P * c + P], hidden[:, P * c:P * c + P], ident)
                        if c == 0:
                            last.then_inc(free, 1)
                    last.then_inc(s["hidT_ps"], 1)
                    pe.wait_ge(s["hidT_sb"], n + 1)
                    for i in range(4):
                        if i:
                            stay_warm(5, 10)
                        w_u = unit_in(q * QUAD_UNITS + 8 + i)
                        for half in range(2):
                            last = strips(6 + half, hiddenT[:, i, :], w_u, half, i == 0, i == 3,
                                          half == 0 and i > 0)
                    last.then_inc(s["down_ps"], 1)
                    pe.wait_ge(s["down_act"], n + 1)
                    pe.wait_ge(s["down_vec"], n + 1)
                    for t in range(TILES):
                        for half in range(2):
                            last = pe.matmul(psum[:, 2 * t + half, :], scatterT[:, t * P:(t + 1) * P],
                                             down_sb[:, 512 * half:512 * half + 512], start=False, stop=False,
                                             skip_group_check=True)
                            if t + half == 0:
                                last.then_inc(free, 1)
                        last.then_inc(s["scattered"], 1)

            pe.wait_ge(normed, 2)
            moe_step(0, main_s, slot_in, ring_free, 0, first_quad=True)
            with pe.Fori(1, STEPS) as step:
                moe_step(step, main_s, slot_in, ring_free, 0)
            pe.wait_ge(routed, 1)
            with pe.If(pe.value_load(most_int[0:1, 0:1], min_val=0, max_val=SEQ) > SLOTS):
                with pe.Fori(0, PASSES - 1) as again:
                    with pe.Fori(0, STEPS) as step:
                        moe_step(again * STEPS + step, more_s, more_in, more_free, FIRST_EXPERT_UNIT)
                pe.nop()

            for t in range(TILES):
                turn(2, t, x_sb)
            w_g = []
            gate_positions = range(FIRST_EXPERT_UNIT + EXPERT_UNITS, FIRST_EXPERT_UNIT + EXPERT_UNITS + 2)
            for n in gate_positions:
                w_g.append(unit(n % RING).rearrange("p (c n) -> p c n", c=4))
            for n, (t, lo, hi, bank) in enumerate(PIECES):
                if n >= 4:
                    pe.wait_ge(opened, n - 3)
                pe.wait_ge(turned_vec, 5 + t)
                for c in range(8):
                    if c == 4:
                        pe.wait_ge(turned_act, 5 + t)
                    if n == 0 and c % 4 == 0:
                        at = gate_positions[c // 4]
                        pe.wait_ge(slot_in[at % RING], 16 * (at // RING + 1))
                    last = pe.matmul(psum[:, bank, 0:hi - lo],
                                     gateT[:, c, t * P:(t + 1) * P], w_g[c // 4][:, c % 4, lo:hi],
                                     start=(c == 0), stop=(c == 7))
                last.then_inc(open_ps, 1)


def constant_table():
    import math
    table = np.zeros((P, C_KEPT + SEQ), np.float32)
    table[:, C_IDENT:C_IDENT + P] = np.eye(P)
    table[:, C_EARLIER:C_EARLIER + P] = np.triu(np.ones((P, P)), 1)
    table[:, C_ONES:C_ONES + P] = 1.0
    table[:, C_SLOT:C_SLOT + SLOTS] = np.arange(SLOTS)
    table[:, C_FIRST:C_FIRST + EXPERTS] = EXPERTS - np.arange(EXPERTS)
    for g, w in enumerate(POOL_WINDOWS):
        table[:, C_EDGE + PAD * g:C_EDGE + PAD * (g + 1)] = 1.0 / np.minimum(np.arange(PAD) + 1, w)
    table[:, C_FLIP:C_FLIP + P] = np.eye(P)[::-1]
    distance = SEQ - 1 - np.arange(SEQ)
    exact = BUCKETS // 2
    far = np.log(np.maximum(distance, 1).astype(np.float32) / np.float32(exact))
    far = far / np.float32(math.log(MAX_DIST / exact)) * np.float32(BUCKETS - exact)
    bucket = np.where(distance < exact, distance, np.minimum(exact + far.astype(np.int32), BUCKETS - 1))
    table[bucket, C_KEPT + np.arange(SEQ)] = 1.0
    return table


INPUTS = ["x", "p", "g_mix", "w_in", "w_pool", "pool_scale", "w_out", "rel_bias", "g_ffn", "w_r1", "b_r1", "w_r2",
          "b_r2", "w_gate", "w_up", "w_down", "g_ple", "w_ple_proj", "w_ple_gate", "g_final"]


def kernel(**inputs):
    import concourse.bacc as bacc
    from concourse.bass_utils import run_bass_kernel_spmd

    nc = bacc.Bacc("TRN2", target_bir_lowering=False, num_devices=1)
    arrays, aps = {}, {}
    for name in [*INPUTS, "consts"]:
        array = constant_table() if name == "consts" else np.ascontiguousarray(inputs[name])
        arrays[f"in_{name}"] = array
        aps[name] = nc.dram_tensor(f"in_{name}", array.shape, mybir.dt.from_np(array.dtype), kind="ExternalInput").ap()
    out = nc.dram_tensor("out_x", (1, SEQ, D), F32, kind="ExternalOutput").ap()
    layer_kernel(nc, aps, out)
    result = run_bass_kernel_spmd(nc, [arrays], core_ids=[0])
    return result.results[0]["out_x"]
```
